# Optimizing a Trainium2 kernel written in Bass

```python
import math
import jax, jax.numpy as jnp
from jax import lax
import numpy as np

D_MODEL = 1024
BATCH = 1
SEQ = 512
DEPTH = 2

HEAD_DIM = 64
SWA_HEADS = 6
SWA_WIDTH = SWA_HEADS * HEAD_DIM
DILATED_BRANCHES = ((128, 1), (512, 4), (2048, 16))
SWA_BLOCK = 128
S5_CHANNELS = 256
S5_GROUP = 16
S5_GROUPS = S5_CHANNELS // S5_GROUP
S5_STATE = 64
S5_DT_MIN = 1e-3
S5_DT_MAX = 1e-1
MLA_HEADS = 6
MLA_NOPE = 64
MLA_ROPE = 32
MLA_QK = MLA_NOPE + MLA_ROPE
MLA_V = 64
MLA_WIDTH = MLA_HEADS * MLA_V
MLA_Q_LORA = 256
MLA_KV_LORA = 128
ROPE_THETA = 10000.0
ATTN_BLOCK = 128
D_MIX = SWA_WIDTH + S5_CHANNELS + MLA_WIDTH
IN_SPLITS = (SWA_WIDTH, SWA_WIDTH, SWA_WIDTH, S5_CHANNELS, MLA_Q_LORA, MLA_KV_LORA, MLA_ROPE)
IN_COLS = 3 * SWA_WIDTH + S5_CHANNELS + MLA_Q_LORA + MLA_KV_LORA + MLA_ROPE
T5_BUCKETS = 32
T5_MAX_DISTANCE = 2048
PEER_KEYS = 128
PEER_EXPERTS = PEER_KEYS * PEER_KEYS
PEER_HEADS = 8
PEER_TOPK = 16
PEER_DKEY = 256
PEER_BLOCK = 128
EPS = 1e-6

kernel_name = "hybrid_swa_s5_mla_peer_trunk"

def rms_norm(x, gain):
    xf = x.astype(jnp.float32)
    y = xf * lax.rsqrt(jnp.mean(xf * xf, axis=-1, keepdims=True) + EPS)
    return (y * gain.astype(jnp.float32)).astype(x.dtype)

def t5_bucket(dist):
    max_exact = T5_BUCKETS // 2
    d_f = jnp.maximum(dist, 1).astype(jnp.float32)
    large = max_exact + (jnp.log(d_f / max_exact) / math.log(T5_MAX_DISTANCE / max_exact)
                         * (T5_BUCKETS - max_exact)).astype(jnp.int32)
    large = jnp.minimum(large, T5_BUCKETS - 1)
    return jnp.where(dist < max_exact, dist, large)

def rope(x, cos, sin):
    half = x.shape[-1] // 2
    x1, x2 = x[..., :half], x[..., half:]
    return jnp.concatenate([x1 * cos - x2 * sin, x1 * sin + x2 * cos], axis=-1)

def dilated_branch(q, k, v, bias_j, dil):
    B, H, S, hd = q.shape
    n_back = bias_j.shape[-1] - 1
    L = S // dil
    nb = -(-L // SWA_BLOCK)
    Lp = nb * SWA_BLOCK

    def to_blocks(t):
        t = t.reshape(B, H, L, dil, hd).transpose(0, 1, 3, 2, 4)
        t = jnp.pad(t, ((0, 0), (0, 0), (0, 0), (0, Lp - L), (0, 0)))
        return t.reshape(B, H, dil, nb, SWA_BLOCK, hd)

    def with_prev(t):
        prev = jnp.pad(t[:, :, :, :-1], ((0, 0), (0, 0), (0, 0), (1, 0), (0, 0), (0, 0)))
        return jnp.concatenate([prev, t], axis=4)

    qb = to_blocks(q)
    kc = with_prev(to_blocks(k))
    vc = with_prev(to_blocks(v)).astype(jnp.float32)
    logits = jnp.einsum('bhrnqd,bhrnkd->bhrnqk', qb, kc).astype(jnp.float32)
    qi = jnp.arange(SWA_BLOCK)[:, None]
    kj = jnp.arange(2 * SWA_BLOCK)[None, :]
    delta = SWA_BLOCK + qi - kj
    band = (delta >= 0) & (delta <= n_back)
    has_prev = (jnp.arange(nb)[:, None, None] > 0) | (kj >= SWA_BLOCK)[None]
    valid = band[None] & has_prev
    bias = bias_j.astype(jnp.float32)[:, jnp.clip(delta, 0, n_back)]
    logits = jnp.where(valid, logits + bias[:, None, None], -jnp.inf)
    mx = jnp.max(logits, axis=-1)
    p = jnp.exp(logits - mx[..., None])
    den = jnp.sum(p, axis=-1)
    num = jnp.einsum('bhrnqk,bhrnkd->bhrnqd', p, vc)

    def from_blocks(t):
        t = t.reshape((B, H, dil, Lp) + t.shape[5:])[:, :, :, :L]
        t = jnp.swapaxes(t, 2, 3)
        return t.reshape((B, H, S) + t.shape[4:])

    return from_blocks(num), from_blocks(den), from_blocks(mx)

def dilated_attention(q, k, v, branch_biases):
    nums, dens, mxs = [], [], []
    for (window, dil), bias_j in zip(DILATED_BRANCHES, branch_biases):
        n_i, d_i, m_i = dilated_branch(q, k, v, bias_j, dil)
        nums.append(n_i)
        dens.append(d_i)
        mxs.append(m_i)
    mx = jnp.stack(mxs)
    w = jnp.exp(mx - jnp.max(mx, axis=0, keepdims=True))
    num = jnp.sum(w[..., None] * jnp.stack(nums), axis=0)
    den = jnp.sum(w * jnp.stack(dens), axis=0)
    return num / den[..., None]

def mla_attention(q, k, v):
    B, H, S, _ = q.shape
    nq = S // ATTN_BLOCK
    qb = q.reshape(B, H, nq, ATTN_BLOCK, MLA_QK).transpose(2, 0, 1, 3, 4)
    k_pos = jnp.arange(S)
    vf = v.astype(jnp.float32)

    def block(args):
        qblk, n = args
        logits = jnp.einsum('bhqd,bhkd->bhqk', qblk, k).astype(jnp.float32)
        q_pos = n * ATTN_BLOCK + jnp.arange(ATTN_BLOCK)
        logits = jnp.where(k_pos[None, :] <= q_pos[:, None], logits, -jnp.inf)
        p = jax.nn.softmax(logits, axis=-1)
        return jnp.einsum('bhqk,bhkd->bhqd', p, vf)

    out = lax.map(block, (qb, jnp.arange(nq)))
    return out.transpose(1, 2, 0, 3, 4).reshape(B, H, S, MLA_V)

def s5_combine(e1, e2):
    a1r, a1i, b1r, b1i = e1
    a2r, a2i, b2r, b2i = e2
    return (a2r * a1r - a2i * a1i,
            a2r * a1i + a2i * a1r,
            a2r * b1r - a2i * b1i + b2r,
            a2r * b1i + a2i * b1r + b2i)

def s5_mixer(u, a_re, a_im, b_re, b_im, c_re, c_im, d_skip, log_dt, w_glu, b_glu):
    B, S, _ = u.shape
    f32 = jnp.float32
    uf = u.astype(f32)
    ug = uf.reshape(B, S, S5_GROUPS, S5_GROUP)
    a_re, a_im = a_re.astype(f32), a_im.astype(f32)
    b_re, b_im = b_re.astype(f32), b_im.astype(f32)
    dt = jnp.exp(log_dt.astype(f32))[:, None]
    mag = jnp.exp(a_re * dt)
    lam_re, lam_im = mag * jnp.cos(a_im * dt), mag * jnp.sin(a_im * dt)
    den = a_re * a_re + a_im * a_im
    nr, ni = lam_re - 1.0, lam_im
    coef_re = (nr * a_re + ni * a_im) / den
    coef_im = (ni * a_re - nr * a_im) / den
    bb_re = coef_re[..., None] * b_re - coef_im[..., None] * b_im
    bb_im = coef_re[..., None] * b_im + coef_im[..., None] * b_re
    bu_re = jnp.einsum('gpc,bsgc->bsgp', bb_re, ug)
    bu_im = jnp.einsum('gpc,bsgc->bsgp', bb_im, ug)
    shape = bu_re.shape
    elems = (jnp.broadcast_to(lam_re, shape), jnp.broadcast_to(lam_im, shape), bu_re, bu_im)
    _, _, xr, xi = lax.associative_scan(s5_combine, elems, axis=1)
    y = (jnp.einsum('gcp,bsgp->bsgc', c_re.astype(f32), xr)
         - jnp.einsum('gcp,bsgp->bsgc', c_im.astype(f32), xi))
    y = y.reshape(B, S, S5_CHANNELS) + d_skip.astype(f32) * uf
    g = jax.nn.gelu(y)
    return g * jax.nn.sigmoid(g @ w_glu.astype(f32) + b_glu.astype(f32))

def token_mixer(h, w_in, w_out, mix_gain, swa_q_gain, swa_k_gain, branch_biases,
                mla_q_lora_gain, mla_kv_lora_gain, w_uq, w_ukv, mla_q_gain, mla_k_gain,
                cos, sin, s5_params):
    B, S, _ = h.shape
    proj = h @ w_in
    cuts = [sum(IN_SPLITS[:i + 1]) for i in range(len(IN_SPLITS) - 1)]
    qa, ka, va, u, cq, ckv, kr = jnp.split(proj, cuts, axis=-1)

    def heads(t, n):
        return t.reshape(B, S, n, -1).transpose(0, 2, 1, 3)
    qa = rms_norm(heads(qa, SWA_HEADS), swa_q_gain) * (HEAD_DIM ** -0.5)
    ka = rms_norm(heads(ka, SWA_HEADS), swa_k_gain)
    ya = dilated_attention(qa, ka, heads(va, SWA_HEADS), branch_biases)
    ya = ya.transpose(0, 2, 1, 3).reshape(B, S, SWA_WIDTH)

    yb = s5_mixer(u, *s5_params)

    q = (rms_norm(cq, mla_q_lora_gain) @ w_uq).reshape(B, S, MLA_HEADS, MLA_QK)
    kv = (rms_norm(ckv, mla_kv_lora_gain) @ w_ukv).reshape(B, S, MLA_HEADS, MLA_NOPE + MLA_V)
    k_nope, vc = kv[..., :MLA_NOPE], kv[..., MLA_NOPE:]
    q_nope = rms_norm(q[..., :MLA_NOPE], mla_q_gain[:MLA_NOPE])
    q_rope = rope(rms_norm(q[..., MLA_NOPE:], mla_q_gain[MLA_NOPE:]), cos, sin)
    k_nope = rms_norm(k_nope, mla_k_gain[:MLA_NOPE])
    k_rope = rope(rms_norm(kr[:, :, None, :], mla_k_gain[MLA_NOPE:]), cos, sin)
    qc = jnp.concatenate([q_nope, q_rope], axis=-1) * (MLA_QK ** -0.5)
    kc = jnp.concatenate([k_nope, jnp.broadcast_to(k_rope, (B, S, MLA_HEADS, MLA_ROPE))], axis=-1)
    yc = mla_attention(qc.transpose(0, 2, 1, 3), kc.transpose(0, 2, 1, 3), vc.transpose(0, 2, 1, 3))
    yc = yc.transpose(0, 2, 1, 3).reshape(B, S, MLA_WIDTH)

    y = jnp.concatenate([
        rms_norm(ya, mix_gain[:SWA_WIDTH]),
        rms_norm(yb, mix_gain[SWA_WIDTH:SWA_WIDTH + S5_CHANNELS]),
        rms_norm(yc, mix_gain[SWA_WIDTH + S5_CHANNELS:]),
    ], axis=-1)
    return y @ w_out

def peer_ffn(h, wq, subkeys, u_tab, v_tab):
    B, S, D = h.shape
    T = B * S
    hf = h.reshape(T, D)
    q = (hf @ wq).reshape(T, PEER_HEADS, 2, PEER_DKEY // 2)
    scores = jnp.einsum('thjd,hjkd->thjk', q, subkeys).astype(jnp.float32)
    top_s, top_i = lax.top_k(scores, PEER_TOPK)
    cand = top_s[:, :, 0, :, None] + top_s[:, :, 1, None, :]
    best_s, best_c = lax.top_k(cand.reshape(T, PEER_HEADS, PEER_TOPK * PEER_TOPK), PEER_TOPK)
    i1 = jnp.take_along_axis(top_i[:, :, 0], best_c // PEER_TOPK, axis=-1)
    i2 = jnp.take_along_axis(top_i[:, :, 1], best_c % PEER_TOPK, axis=-1)
    nblk = T // PEER_BLOCK
    experts = (i1 * PEER_KEYS + i2).reshape(nblk, PEER_BLOCK, PEER_HEADS * PEER_TOPK)
    gates = jax.nn.softmax(best_s, axis=-1).reshape(nblk, PEER_BLOCK, PEER_HEADS * PEER_TOPK)
    xb = hf.reshape(nblk, PEER_BLOCK, D)

    def block(args):
        xt, et, gt = args
        act = jax.nn.gelu(jnp.einsum('td,tkd->tk', xt, u_tab[et]).astype(jnp.float32))
        return jnp.einsum('tk,tkd->td', gt * act, v_tab[et].astype(jnp.float32))

    out = lax.map(block, (xb, experts, gates))
    return out.reshape(B, S, D)

def setup_inputs(seed: int = 0) -> dict:
    key = jax.random.key(seed)
    ks = jax.random.split(key, 40)
    f32 = jnp.float32

    def nrm(k, shape, scale):
        return jax.random.normal(k, shape, f32) * scale

    def gain(k, shape):
        return 1.0 + 0.02 * jax.random.normal(k, shape, f32)

    L, D = DEPTH, D_MODEL
    return {
        "x": nrm(ks[0], (BATCH, SEQ, D), 1.0),
        "c": nrm(ks[1], (BATCH, D), 1.0),
        "w_in": nrm(ks[2], (L, D, IN_COLS), D ** -0.5),
        "w_out": nrm(ks[3], (L, D_MIX, D), D_MIX ** -0.5),
        "mix_gain": gain(ks[4], (L, D_MIX)),
        "norm1_gain": gain(ks[5], (L, D)),
        "norm2_gain": gain(ks[6], (L, D)),
        "w_ada": nrm(ks[7], (L, D, 6 * D), 0.5 * D ** -0.5),
        "b_ada": nrm(ks[8], (L, 6 * D), 0.02),
        "rel_bias": nrm(ks[9], (SWA_HEADS, T5_BUCKETS), 0.5),
        "swa_q_gain": gain(ks[10], (L, HEAD_DIM)),
        "swa_k_gain": gain(ks[11], (L, HEAD_DIM)),
        "mla_q_lora_gain": gain(ks[12], (L, MLA_Q_LORA)),
        "mla_kv_lora_gain": gain(ks[13], (L, MLA_KV_LORA)),
        "w_uq": nrm(ks[14], (L, MLA_Q_LORA, MLA_HEADS * MLA_QK), MLA_Q_LORA ** -0.5),
        "w_ukv": nrm(ks[15], (L, MLA_KV_LORA, MLA_HEADS * (MLA_NOPE + MLA_V)), MLA_KV_LORA ** -0.5),
        "mla_q_gain": gain(ks[16], (L, MLA_QK)),
        "mla_k_gain": gain(ks[17], (L, MLA_QK)),
        "s5_a_re": -0.5 + nrm(ks[18], (L, S5_GROUPS, S5_STATE), 0.01),
        "s5_a_im": math.pi * jnp.arange(S5_STATE, dtype=f32) + nrm(ks[19], (L, S5_GROUPS, S5_STATE), 0.01),
        "s5_b_re": nrm(ks[20], (L, S5_GROUPS, S5_STATE, S5_GROUP), (2 * S5_GROUP) ** -0.5),
        "s5_b_im": nrm(ks[21], (L, S5_GROUPS, S5_STATE, S5_GROUP), (2 * S5_GROUP) ** -0.5),
        "s5_c_re": nrm(ks[22], (L, S5_GROUPS, S5_GROUP, S5_STATE), (2 * S5_STATE) ** -0.5),
        "s5_c_im": nrm(ks[23], (L, S5_GROUPS, S5_GROUP, S5_STATE), (2 * S5_STATE) ** -0.5),
        "s5_d": nrm(ks[24], (L, S5_CHANNELS), 1.0),
        "s5_log_dt": jax.random.uniform(ks[25], (L, S5_GROUPS), f32, math.log(S5_DT_MIN), math.log(S5_DT_MAX)),
        "w_glu": nrm(ks[26], (L, S5_CHANNELS, S5_CHANNELS), S5_CHANNELS ** -0.5),
        "b_glu": nrm(ks[27], (L, S5_CHANNELS), 0.02),
        "peer_wq": nrm(ks[28], (L, D, PEER_HEADS * PEER_DKEY), D ** -0.5),
        "peer_subkeys": nrm(ks[29], (L, PEER_HEADS, 2, PEER_KEYS, PEER_DKEY // 2), (PEER_DKEY // 2) ** -0.5),
        "peer_u": nrm(ks[30], (L, PEER_EXPERTS, D), D ** -0.5),
        "peer_v": nrm(ks[31], (L, PEER_EXPERTS, D), 0.5),
    }

def reference(x, c, w_in, w_out, mix_gain, norm1_gain, norm2_gain, w_ada, b_ada, rel_bias,
              swa_q_gain, swa_k_gain, mla_q_lora_gain, mla_kv_lora_gain, w_uq, w_ukv,
              mla_q_gain, mla_k_gain, s5_a_re, s5_a_im, s5_b_re, s5_b_im, s5_c_re, s5_c_im,
              s5_d, s5_log_dt, w_glu, b_glu, peer_wq, peer_subkeys, peer_u, peer_v):
    B, S, _ = x.shape
    f32 = jnp.float32
    pos = jnp.arange(S, dtype=f32)
    inv_freq = ROPE_THETA ** (-jnp.arange(0, MLA_ROPE, 2, dtype=f32) / MLA_ROPE)
    ang = pos[:, None] * inv_freq[None, :]
    cos, sin = jnp.cos(ang)[:, None, :], jnp.sin(ang)[:, None, :]
    branch_biases = [rel_bias[:, t5_bucket(dil * jnp.arange(window // dil + 1))]
                     for window, dil in DILATED_BRANCHES]
    c_act = jax.nn.silu(c)
    for l in range(DEPTH):
        mod = c_act @ w_ada[l] + b_ada[l]
        sh1, sc1, g1, sh2, sc2, g2 = jnp.split(mod, 6, axis=-1)
        h = rms_norm(x, norm1_gain[l]) * (1.0 + sc1[:, None]) + sh1[:, None]
        s5_params = (s5_a_re[l], s5_a_im[l], s5_b_re[l], s5_b_im[l], s5_c_re[l], s5_c_im[l],
                     s5_d[l], s5_log_dt[l], w_glu[l], b_glu[l])
        y = token_mixer(h, w_in[l], w_out[l], mix_gain[l], swa_q_gain[l], swa_k_gain[l], branch_biases,
                        mla_q_lora_gain[l], mla_kv_lora_gain[l], w_uq[l], w_ukv[l],
                        mla_q_gain[l], mla_k_gain[l], cos, sin, s5_params)
        x = x + g1[:, None] * y
        h = rms_norm(x, norm2_gain[l]) * (1.0 + sc2[:, None]) + sh2[:, None]
        x = x + g2[:, None] * peer_ffn(h, peer_wq[l], peer_subkeys[l], peer_u[l], peer_v[l])
    return x


_drawn_inputs = setup_inputs


def setup_inputs(seed=0):
    import zlib

    import numpy as np

    out = dict(_drawn_inputs(seed))
    spreads = {}
    factors = {'mix_gain': 4.448,
     'norm1_gain': 4.609,
     'norm2_gain': 3.427,
     'swa_q_gain': 8.0,
     'swa_k_gain': 8.0,
     'mla_q_lora_gain': 8.0,
     'mla_kv_lora_gain': 5.399,
     'mla_q_gain': 8.0,
     'mla_k_gain': 8.0,
     's5_a_re': 8.0,
     's5_a_im': 2.747,
     's5_b_re': 3.467,
     's5_b_im': 3.448,
     's5_c_re': 3.551,
     's5_c_im': 3.431,
     's5_log_dt': 3.173,
     'b_glu': 8.0}
    for name, (base, spread) in spreads.items():
        noise = np.random.default_rng([zlib.crc32(name.encode()), seed]).standard_normal(out[name].shape)
        drawn = base * np.exp(spread * noise) if base else spread * noise
        out[name] = __import__('jax').numpy.asarray(drawn.astype(out[name].dtype))
    for name, factor in factors.items():
        out[name] = (out[name] * factor).astype(out[name].dtype)
    return out
```

```python
import math
from contextlib import ExitStack

import numpy as np

import concourse.bass as bass
from concourse import mybir

ALU = mybir.AluOpType
ACT = mybir.ActivationFunctionType
AX = mybir.AxisListType
F32 = mybir.dt.float32
I32 = mybir.dt.int32
U32 = mybir.dt.uint32

P = 128
D = 1024
KD = D // P
S = 512
T = S // P
DEPTH = 2
HEADS = 6
HD = 64
SWA = HEADS * HD
S5C = 256
GROUPS = 16
STATE = 64
GC = 16
SJ = GROUPS * STATE // P
NOPE = 64
ROPE = 32
QK = NOPE + ROPE
QLORA = 256
KVLORA = 128
COLS = 3 * SWA + S5C + QLORA + KVLORA + ROPE
U0 = 3 * SWA
CQ0 = U0 + S5C
CKV0 = CQ0 + QLORA
KR0 = CKV0 + KVLORA
KEYS = 128
EXPERTS = KEYS * KEYS
PH = 8
TOPK = 16
SLOTS = PH * TOPK
RING = 8
CREDIT = RING + 1
EPS = 1e-6
BUCKETS = 32
MAXDIST = 2048
BRANCHES = ((128, 1), (512, 4), (2048, 16))
NEG = -1e30
LOWEST = -3e38
GELU_C = 2.0 * math.sqrt(2.0 / math.pi)
ROUND = 1.5 * 2.0 ** 23
ROUND13 = 1.5 * 2.0 ** 10
TWO_PI = 6.283185
TOEP = 640


def constants():
    dist = S - 1 - np.arange(TOEP)
    large = 16 + (np.log(np.maximum(dist, 1).astype(np.float32) / np.float32(16))
                  / np.float32(math.log(MAXDIST / 16)) * np.float32(16)).astype(np.int32)
    bucket = np.where(dist < 16, dist, np.minimum(large, BUCKETS - 1))
    mult = sum(((dist >= 0) & (dist % dil == 0) & (dist <= window)).astype(np.float32)
               for window, dil in BRANCHES)
    rows = np.zeros((BUCKETS + 2, TOEP), np.float32)
    for b in range(BUCKETS):
        rows[b] = (bucket == b) & (dist >= 0)
    rows[BUCKETS] = np.where(mult > 0, np.log(np.maximum(mult, 1)), NEG)
    rows[BUCKETS + 1] = np.where(dist >= 0, 0.0, NEG)
    sel = np.zeros((BUCKETS + 2, HEADS + 1), np.float32)
    sel[BUCKETS, :HEADS] = 1.0
    sel[BUCKETS + 1, HEADS] = 1.0
    inv_freq = np.float32(10000.0) ** (-np.arange(0, ROPE, 2, dtype=np.float32) / np.float32(ROPE))
    ang = np.arange(S, dtype=np.float32)[:, None] * inv_freq.astype(np.float32)[None, :]
    states = np.arange(P)
    blk = np.zeros((P, SJ, 8), np.float32)
    for j in range(SJ):
        blk[states, j, (2 * j + states // STATE) % 8] = 1.0
    rowpar = np.zeros((P, P), np.float32)
    for r in range(P):
        half = (r // GC) % 2
        rowpar[r, half * STATE:(half + 1) * STATE] = 1.0
    means = np.zeros((P, 16), np.float32)
    means[:, :12] = 1.0 / HD
    means[:, 12] = 1.0 / QLORA
    means[:, 13] = 1.0 / KVLORA
    means[:, 14] = 1.0 / ROPE
    means[:, 15] = 1.0
    return {
        "c_rows": rows, "c_sel": sel,
        "c_eye": np.eye(P, dtype=np.float32), "c_flip": np.eye(P, dtype=np.float32)[::-1].copy(),
        "c_cos": np.cos(ang).astype(np.float32), "c_sin": np.sin(ang).astype(np.float32),
        "c_blk": blk.reshape(P, SJ * 8), "c_rowpar": rowpar, "c_means": means,
        "c_steps": np.broadcast_to(np.arange(1, S + 1, dtype=np.float32), (P, S)).copy(),
        "c_list": np.broadcast_to(np.arange(TOPK, dtype=np.float32), (P, TOPK)).copy(),
    }


class Link:

    def __init__(self, eng, own):
        self.eng, self.own, self.count = eng, own, {}

    def mark(self, ins, sem=None):
        sem = sem or self.own
        n = self.count[sem.name] = self.count.get(sem.name, 0) + 1
        ins.then_inc(sem, 1)
        return n

    def __call__(self, ins, sem=None):
        n = self.mark(ins, sem)
        self.eng.wait_ge(sem or self.own, n)


def gelu_terms(link, dve, y, g, cap=80.0):
    link(dve.tensor_tensor(g, y, y, ALU.mult))
    link(dve.tensor_scalar(g, g, 0.044715, 1.0, ALU.mult, ALU.add))
    link(dve.tensor_tensor(g, g, y, ALU.mult))
    link(dve.tensor_scalar(g, g, -GELU_C, cap, ALU.mult, ALU.min))


def s5_block(nc, a, layer, link, sem_of, PS, PRJ, H, HT, eye, blk, rowpar):
    with ExitStack() as st:
        def sb(name, shape, dt=F32):
            return st.enter_context(nc.sbuf_tensor(name, shape, dt))

        steps = sb("steps", [P, S])
        UT = sb("UT", [P, 2, S])
        BR = sb("BR", [P, SJ, GC])
        BI = sb("BI", [P, SJ, GC])
        BB = sb("BB", [P, 2, SJ, GC])
        BT = sb("BT", [P, SJ, GC])
        BP = sb("BP", [P, 2, SJ, P])
        BW = sb("BW", [P, 2, SJ, P])
        CP = sb("CP", [P, 2, 2, 2, STATE])
        CW = sb("CW", [P, 3, SJ, 32])
        K = sb("K", [P, 20, SJ])
        F = sb("F", [P, 3, S])
        FT = sb("FT", [P, 2, S])
        SN = sb("SN", [P, 2, S])
        CS = sb("CS", [P, 2, S])
        Z, QQ = HT[:, 0:4, :], HT[:, 6:8, :]
        PR = sb("PR", [P, 2, 4, S])
        DG = sb("DG", [P, 2, S5C])
        WG = sb("WG", [P, 2, S5C])
        Y = sb("Y", [P, T, S5C])
        G = HT[:, 4:6, :].rearrange("p a (b c) -> p (a b) c", c=S5C)
        GT = sb("GT", [P, 2, S])
        ar, ai, ldt, dt, mag, w, tmp, sn, s2, cs, lr, li, den, cr, ci, t2, whi, wlo, acts, mdt = (
            K[:, i, :] for i in range(20))
        (loads, gate_in, ut_tp, ut_ev, k_act, k_dve, pad, bw_tp, bw_ev, cw_ready, phase, tab, tab_used, bu_mm,
         prod, y_mm, y_ready, e_ready, g_ready, gt_tp, gt_ev, glu_mm, glu_pre, glu_e, rotated, f_used) = (
            sem_of(f"s5_{s}") for s in
            ("loads", "gate_in", "ut_tp", "ut_ev", "k_act", "k_dve", "pad", "bw_tp", "bw_ev", "cw_ready", "phase",
             "tab", "tab_used", "bu_mm", "prod", "y_mm", "y_ready", "e_ready", "g_ready", "gt_tp", "gt_ev",
             "glu_mm", "glu_pre", "glu_e", "rotated", "f_used"))
        act_step, pool_step = sem_of("s5_act_step"), sem_of("s5_pool_step")
        n_loads = 0
        with nc.Block() as block:
            @block.sync
            def _(sp):
                nonlocal n_loads
                col = dict(allow_slow_non_contiguous=True)

                def load(dst, src, **k):
                    nonlocal n_loads
                    n_loads += 1
                    sp.dma_start(dst, src, **k).then_inc(loads, 16)

                load(ar, a["s5_a_re"][layer].rearrange("(j g) p -> (g p) j", g=2), **col)
                load(ai, a["s5_a_im"][layer].rearrange("(j g) p -> (g p) j", g=2), **col)
                for half in range(2):
                    load(ldt[half * STATE:(half + 1) * STATE, :],
                         a["s5_log_dt"][layer].rearrange("(j g) -> g j", g=2)[half, :].partition_broadcast(STATE),
                         **col)
                load(BR[:, :, :], a["s5_b_re"][layer].rearrange("(j g) p c -> (g p) j c", g=2))
                load(BI[:, :, :], a["s5_b_im"][layer].rearrange("(j g) p c -> (g p) j c", g=2))
                for i, name in enumerate(("s5_c_re", "s5_c_im")):
                    src = a[name][layer].rearrange("(h g) c p -> (g c) h p", h=2)
                    for copy in range(2):
                        load(CP[:, i, :, copy, :], src)
                load(steps[:, :], a["c_steps"])
                sp.dma_start(DG[:, 0, :], a["s5_d"][layer, :].partition_broadcast(P)).then_inc(gate_in, 16)
                sp.dma_start(DG[:, 1, :], a["b_glu"][layer, :].partition_broadcast(P)).then_inc(gate_in, 16)
                sp.dma_start(WG[:, :, :], a["w_glu"][layer].rearrange("(k p) n -> p k n", p=P)).then_inc(gate_in, 16)

            @block.gpsimd
            def _(pool):
                slink = Link(pool, pool_step)
                pool.wait_ge(k_dve, 3)
                for j in range(SJ):
                    A, R, B = (F[:, i, :] for i in range(3))
                    ft = FT[:, j % 2, :]
                    slink(pool.tensor_scalar(A, steps[:, :], whi[:, j:j + 1], None, ALU.mult))
                    slink(pool.tensor_scalar(R, A, ROUND, None, ALU.add))
                    slink(pool.tensor_scalar(R, R, ROUND, None, ALU.subtract))
                    slink(pool.tensor_tensor(A, A, R, ALU.subtract))
                    slink(pool.tensor_scalar(B, steps[:, :], wlo[:, j:j + 1], None, ALU.mult))
                    slink(pool.tensor_tensor(A, A, B, ALU.add))
                    slink(pool.tensor_scalar(R, A, ROUND, None, ALU.add))
                    slink(pool.tensor_scalar(R, R, ROUND, None, ALU.subtract))
                    if j >= 2:
                        pool.wait_ge(f_used, 2 * (j - 1))
                    slink(pool.tensor_tensor(ft, A, R, ALU.subtract), phase)

            @block.scalar
            def _(act):
                slink = Link(act, act_step)
                act.wait_ge(loads, 16 * n_loads)
                slink(act.activation(dt, ldt, ACT.Exp))
                act.activation(mdt, dt, ACT.Copy).then_inc(k_act, 1)
                act.wait_ge(k_dve, 1)
                act.activation(mag, tmp, ACT.Exp).then_inc(k_act, 1)
                act.wait_ge(k_dve, 2)
                act.activation(sn, w, ACT.Sin, scale=TWO_PI).then_inc(k_act, 1)
                act.activation(s2, w, ACT.Sin, scale=TWO_PI / 2).then_inc(k_act, 1)
                for i in range(2):
                    act.wait_ge(ut_tp, i + 1)
                    act.activation(UT[:, i, :], PS[:, 6 + i, :], ACT.Copy).then_inc(ut_ev, 1)
                for i in range(16):
                    act.wait_ge(bw_tp, i + 1)
                    act.activation(BW[:, i // SJ, i % SJ, :], PS[:, 4 + i % 4, 0:P], ACT.Copy).then_inc(bw_ev, 1)
                for i in range(4):
                    act.wait_ge(bw_tp, 17 + i)
                    part, h = i // 2, i % 2
                    src = PS[:, 4 + i % 4, 0:P].rearrange("p (j c) -> p j c", c=32)
                    if part == 0:
                        act.activation(CW[:, 0, 4 * h:4 * h + 4, :], src, ACT.Copy).then_inc(cw_ready, 1)
                        act.activation(CW[:, 1, 4 * h:4 * h + 4, :], src, ACT.Copy, scale=-1.0).then_inc(cw_ready, 1)
                    else:
                        act.activation(CW[:, 2, 4 * h:4 * h + 4, :], src, ACT.Copy, scale=-1.0).then_inc(cw_ready, 1)
                for j in range(SJ):
                    b = j % 2
                    act.wait_ge(phase, j + 1)
                    if j >= 2:
                        act.wait_ge(tab_used, j - 1)
                    act.activation(SN[:, b, :], FT[:, b, :], ACT.Sin, scale=TWO_PI).then_inc(f_used, 1)
                    act.activation(QQ[:, 0, :], FT[:, b, :], ACT.Sin, scale=TWO_PI / 2).then_inc(f_used, 1)
                    act.wait_ge(f_used, 2 * j + 2)
                    slink(act.activation(QQ[:, 1, :], QQ[:, 0, :], ACT.Square, scale=math.sqrt(2.0)))
                    act.activation(CS[:, b, :], QQ[:, 1, :], ACT.Copy, scale=-1.0, bias=1.0).then_inc(tab, 1)
                    act.wait_ge(tab, j + 1)
                act.wait_ge(y_ready, 1)
                act.activation(G[:, :, :], G[:, :, :], ACT.Exp).then_inc(e_ready, 1)
                for i in range(2):
                    act.wait_ge(gt_tp, i + 1)
                    act.activation(GT[:, i, :], PS[:, 6 + i, :], ACT.Copy).then_inc(gt_ev, 1)
                act.wait_ge(glu_pre, 1)
                act.activation(G[:, :, :], G[:, :, :], ACT.Exp, scale=-1.0).then_inc(glu_e, 1)

            @block.tensor
            def _(pe):
                for i in range(2):
                    for t in range(T):
                        last = pe.transpose(PS[:, 6 + i, t * P:(t + 1) * P], PRJ[:, t, U0 + i * P:U0 + (i + 1) * P],
                                            eye[:, :])
                    last.then_inc(ut_tp, 1)
                pe.wait_ge(ut_ev, 2)
                pe.wait_ge(pad, 2)
                for i in range(16):
                    if i >= 4:
                        pe.wait_ge(bw_ev, i - 3)
                    pe.transpose(PS[:, 4 + i % 4, 0:P], BP[:, i // SJ, i % SJ, :], eye[:, :]).then_inc(bw_tp, 1)
                pe.wait_ge(pad, 3)
                for i in range(4):
                    pe.wait_ge(bw_ev, 13 + i)
                    pe.transpose(PS[:, 4 + i % 4, 0:P], CP[:, i // 2, i % 2, :, :].rearrange("p a b -> p (a b)"),
                                 eye[:, :]).then_inc(bw_tp, 1)
                pe.wait_ge(ut_ev, 2)

                def drive(j):
                    if j >= 2:
                        pe.wait_ge(rotated, j - 1)
                    for c in range(2):
                        last = pe.matmul(PS[:, 2 * (j % 2) + c, :], BW[:, c, j, :], UT[:, j // 4, :],
                                         start=True, stop=True)
                    last.then_inc(bu_mm, 1)

                drive(0)
                pe.wait_ge(cw_ready, 6)
                for j in range(SJ):
                    if j + 1 < SJ:
                        drive(j + 1)
                    pe.wait_ge(prod, j + 1)
                    for t in range(T):
                        for q, wt in enumerate((0, 1, 2, 2)):
                            y0 = (t % 2) * S5C + 32 * j
                            last = pe.matmul(PS[:, 4 + t // 2, y0:y0 + 32], PR[:, j % 2, q, t * P:(t + 1) * P],
                                             CW[:, wt, j, :], start=(q == 0), stop=(q == 3))
                    last.then_inc(y_mm, 1)
                pe.wait_ge(g_ready, 1)
                for i in range(2):
                    for t in range(T):
                        last = pe.transpose(PS[:, 6 + i, t * P:(t + 1) * P], Y[:, t, i * P:(i + 1) * P], eye[:, :])
                    last.then_inc(gt_tp, 1)
                pe.wait_ge(gate_in, 48)
                pe.wait_ge(gt_ev, 2)
                for t in range(T):
                    for k in range(2):
                        last = pe.matmul(PS[:, t // 2, (t % 2) * S5C:(t % 2 + 1) * S5C], GT[:, k, t * P:(t + 1) * P],
                                         WG[:, k, :], start=(k == 0), stop=(k == 1))
                last.then_inc(glu_mm, 1)

            @block.vector
            def _(dve):
                link.eng = dve
                dve.wait_ge(k_act, 1)
                link(dve.tensor_tensor(tmp, ar, mdt, ALU.mult), k_dve)
                link(dve.tensor_tensor(w, ai, mdt, ALU.mult))
                link(dve.tensor_scalar(w, w, 1.0 / (2.0 * math.pi), None, ALU.mult))
                link(dve.tensor_scalar(t2, w, ROUND, None, ALU.add))
                link(dve.tensor_scalar(t2, t2, ROUND, None, ALU.subtract))
                link(dve.tensor_tensor(w, w, t2, ALU.subtract), k_dve)
                link(dve.tensor_scalar(whi, w, ROUND13, None, ALU.add))
                link(dve.tensor_scalar(whi, whi, ROUND13, None, ALU.subtract))
                link(dve.tensor_tensor(wlo, w, whi, ALU.subtract), k_dve)
                dve.wait_ge(k_act, 4)
                link(dve.tensor_tensor(cs, s2, s2, ALU.mult))
                link(dve.tensor_scalar(cs, cs, -2.0, 1.0, ALU.mult, ALU.add))
                link(dve.tensor_tensor(lr, mag, cs, ALU.mult))
                link(dve.tensor_scalar(lr, lr, -1.0, None, ALU.add))
                link(dve.tensor_tensor(li, mag, sn, ALU.mult))
                link(dve.tensor_tensor(den, ar, ar, ALU.mult))
                link(dve.tensor_tensor(t2, ai, ai, ALU.mult))
                link(dve.tensor_tensor(den, den, t2, ALU.add))
                link(dve.reciprocal(den, den))
                link(dve.tensor_tensor(cr, lr, ar, ALU.mult))
                link(dve.tensor_tensor(t2, li, ai, ALU.mult))
                link(dve.tensor_tensor(cr, cr, t2, ALU.add))
                link(dve.tensor_tensor(cr, cr, den, ALU.mult))
                link(dve.tensor_tensor(ci, li, ar, ALU.mult))
                link(dve.tensor_tensor(t2, lr, ai, ALU.mult))
                link(dve.tensor_tensor(ci, ci, t2, ALU.subtract))
                link(dve.tensor_tensor(ci, ci, den, ALU.mult))
                crb = cr.unsqueeze(2).to_broadcast([P, SJ, GC])
                cib = ci.unsqueeze(2).to_broadcast([P, SJ, GC])
                link(dve.tensor_tensor(BB[:, 0, :, :], BR[:, :, :], crb, ALU.mult))
                link(dve.tensor_tensor(BT[:, :, :], BI[:, :, :], cib, ALU.mult))
                link(dve.tensor_tensor(BB[:, 0, :, :], BB[:, 0, :, :], BT[:, :, :], ALU.subtract))
                link(dve.tensor_tensor(BB[:, 1, :, :], BI[:, :, :], crb, ALU.mult))
                link(dve.tensor_tensor(BT[:, :, :], BR[:, :, :], cib, ALU.mult))
                link(dve.tensor_tensor(BB[:, 1, :, :], BB[:, 1, :, :], BT[:, :, :], ALU.add))
                for i in range(2):
                    link(dve.tensor_tensor(BP[:, i, :, :].rearrange("p j (b c) -> p j b c", c=GC),
                                           BB[:, i, :, :].unsqueeze(2).to_broadcast([P, SJ, 8, GC]),
                                           blk[:, :, :].unsqueeze(3).to_broadcast([P, SJ, 8, GC]), ALU.mult), pad)
                cp = CP[:, :, :, :, :].rearrange("p i h a b -> p (i h) (a b)")
                link(dve.tensor_tensor(cp, cp, rowpar[:, :].unsqueeze(1).to_broadcast([P, 4, P]), ALU.mult), pad)
                for j in range(SJ):
                    b = j % 2
                    br, bi = PS[:, 2 * b, :], PS[:, 2 * b + 1, :]
                    c, s = CS[:, b, :], SN[:, b, :]
                    z = [Z[:, i, :] for i in range(4)]
                    dve.wait_ge(tab, j + 1)
                    dve.wait_ge(bu_mm, j + 1)
                    link(dve.tensor_tensor(z[0], br, c, ALU.mult))
                    link(dve.tensor_tensor(z[1], bi, s, ALU.mult))
                    link(dve.tensor_tensor(z[0], z[0], z[1], ALU.add))
                    link(dve.tensor_tensor(z[1], bi, c, ALU.mult))
                    link(dve.tensor_tensor(z[2], br, s, ALU.mult), rotated)
                    link(dve.tensor_tensor(z[1], z[1], z[2], ALU.subtract))
                    m = mag[:, j:j + 1].to_broadcast([P, S])
                    link(dve.tensor_tensor_scan(z[2], m, z[0], 0.0, ALU.mult, ALU.add))
                    link(dve.tensor_tensor_scan(z[3], m, z[1], 0.0, ALU.mult, ALU.add))
                    if j >= 2:
                        dve.wait_ge(y_mm, j - 1)
                    link(dve.tensor_tensor(PR[:, b, 0, :], z[2], c, ALU.mult))
                    link(dve.tensor_tensor(PR[:, b, 1, :], z[3], s, ALU.mult))
                    link(dve.tensor_tensor(PR[:, b, 2, :], z[3], c, ALU.mult))
                    link(dve.tensor_tensor(PR[:, b, 3, :], z[2], s, ALU.mult), prod)
                    dve.sem_inc(tab_used, 1)
                dve.wait_ge(gate_in, 48)
                dve.wait_ge(y_mm, SJ)
                u = PRJ[:, :, U0:U0 + S5C]
                link(dve.tensor_tensor(Y[:, :, :], u, DG[:, 0, :].unsqueeze(1).to_broadcast([P, T, S5C]), ALU.mult))
                link(dve.tensor_tensor(Y[:, :, :], Y[:, :, :],
                                       PS[:, 4:6, :].rearrange("p b (t c) -> p (b t) c", c=S5C), ALU.add))
                gelu_terms(link, dve, Y[:, :, :], G[:, :, :])
                dve.sem_inc(y_ready, 1)
                dve.wait_ge(e_ready, 1)
                link(dve.tensor_scalar(G[:, :, :], G[:, :, :], 1.0, None, ALU.add))
                link(dve.reciprocal(G[:, :, :], G[:, :, :]))
                link(dve.tensor_tensor(Y[:, :, :], Y[:, :, :], G[:, :, :], ALU.mult), g_ready)
                dve.wait_ge(glu_mm, 1)
                link(dve.tensor_tensor(G[:, :, :], PS[:, 0:2, :].rearrange("p b (t c) -> p (b t) c", c=S5C),
                                       DG[:, 1, :].unsqueeze(1).to_broadcast([P, T, S5C]), ALU.add))
                link(dve.tensor_scalar(G[:, :, :], G[:, :, :], -80.0, None, ALU.max), glu_pre)
                dve.wait_ge(glu_e, 1)
                link(dve.tensor_scalar(G[:, :, :], G[:, :, :], 1.0, None, ALU.add))
                link(dve.reciprocal(G[:, :, :], G[:, :, :]))
                link(dve.tensor_tensor(H[:, :, SWA:SWA + S5C], Y[:, :, :], G[:, :, :], ALU.mult))


def attention(nc, a, layer, link, sem_of, PS, PRJ, H, HT, eye, means, BM, cosT, sinT, RS, V0, rsqrt):
    with ExitStack() as st:
        def sb(name, shape, dt=F32):
            return st.enter_context(nc.sbuf_tensor(name, shape, dt))

        QM = sb("QM", [P, T, HEADS, QK])
        KC = sb("KC", [P, T, HEADS, QK])
        KV = sb("KV", [P, T, HEADS, NOPE + HD])
        GQK = sb("GQK", [P, 2, HD])
        GM = sb("GM", [P, 2, QK])
        GC_ = sb("GC_", [P, QLORA + KVLORA])
        SQ = HT[:, :, :].rearrange("p k s -> p (k s)")
        gains, w_in, sq, sq2, cn, tp, ev, mm, mev, sq3, sq4 = (sem_of(f"at_{s}") for s in (
            "gains", "w", "sq", "sq2", "cn", "tp", "ev", "mm", "mev", "sq3", "sq4"))
        with ExitStack() as lat:
            WUQ = lat.enter_context(nc.sbuf_tensor("WUQ", [P, 2, HEADS * QK], F32))
            WUKV = lat.enter_context(nc.sbuf_tensor("WUKV", [P, HEADS * (NOPE + HD)], F32))
            CT = lat.enter_context(nc.sbuf_tensor("CT", [P, 3, S], F32))
            with nc.Block() as block:
                @block.sync
                def _(sp):
                    for dst, name in ((GQK[:, 0, :], "swa_q_gain"), (GQK[:, 1, :], "swa_k_gain"),
                                      (GM[:, 0, :], "mla_q_gain"), (GM[:, 1, :], "mla_k_gain"),
                                      (GC_[:, 0:QLORA], "mla_q_lora_gain"), (GC_[:, QLORA:], "mla_kv_lora_gain")):
                        sp.dma_start(dst, a[name][layer, :].partition_broadcast(P)).then_inc(gains, 16)
                    sp.dma_start(WUQ[:, :, :], a["w_uq"][layer].rearrange("(k p) n -> p k n", p=P)).then_inc(w_in, 16)
                    sp.dma_start(WUKV[:, :], a["w_ukv"][layer]).then_inc(w_in, 16)

                @block.scalar
                def _(act):
                    sq_step = sem_of("at_sq_step")
                    for t in range(T):
                        act.activation(SQ[:, t * 768:(t + 1) * 768], PRJ[:, t, 0:768], ACT.Square).then_inc(sq, 1)
                    for t in range(T):
                        for i, (lo, hi) in enumerate(((CQ0, CKV0), (CKV0, KR0), (KR0, COLS))):
                            c = t * 15 + 12 + i
                            if t or i:
                                act.wait_ge(sq2, 3 * t + i)
                            act.activation(SQ[:, 3072:3072 + hi - lo], PRJ[:, t, lo:hi], ACT.Square,
                                           accum_out=V0[:, c:c + 1]).then_inc(sq2, 1)
                    for i in range(3):
                        act.wait_ge(tp, i + 1)
                        act.activation(CT[:, i, :], PS[:, i, :], ACT.Copy).then_inc(ev, 1)
                    for t in range(T):
                        for n in range(4):
                            i = 4 * t + n
                            act.wait_ge(mm, i + 1)
                            if n < 2:
                                act.activation(QM[:, t, 3 * n:3 * n + 3, :], PS[:, 4 + n, 0:3 * QK].rearrange(
                                    "p (h c) -> p h c", c=QK), ACT.Copy).then_inc(mev, 1)
                            else:
                                m = n - 2
                                act.activation(KV[:, t, 3 * m:3 * m + 3, :], PS[:, 4 + n, 0:384].rearrange(
                                    "p (h c) -> p h c", c=P), ACT.Copy).then_inc(mev, 1)

                @block.vector
                def _(dve):
                    link.eng = dve
                    v15 = V0[:, 0:60].rearrange("p (t c) -> p t c", c=15)
                    for t in range(T):
                        dve.wait_ge(sq, t + 1)
                        link(dve.tensor_reduce(v15[:, t, 0:12],
                                               SQ[:, t * 768:(t + 1) * 768].rearrange("p (h c) -> p h c", c=HD),
                                               AX.X, ALU.add))
                    dve.wait_ge(sq2, 12)
                    link(dve.tensor_tensor(v15, v15, means[:, 0:15].unsqueeze(1).to_broadcast([P, T, 15]), ALU.mult))
                    link(dve.tensor_scalar(V0[:, 0:60], V0[:, 0:60], EPS, None, ALU.add))
                    rsqrt(link, 60)
                    r15 = RS[:, 0:60].rearrange("p (t c) -> p t c", c=15)
                    dve.wait_ge(gains, 96)
                    for t in range(T):
                        for lo, hi, c, g in ((CQ0, CKV0, 12, 0), (CKV0, KR0, 13, QLORA)):
                            link(dve.scalar_tensor_tensor(PRJ[:, t, lo:hi], PRJ[:, t, lo:hi],
                                                          RS[:, 15 * t + c:15 * t + c + 1], GC_[:, g:g + hi - lo],
                                                          ALU.mult, ALU.mult), cn)
                        link(dve.scalar_tensor_tensor(PRJ[:, t, KR0:COLS], PRJ[:, t, KR0:COLS],
                                                      RS[:, 15 * t + 14:15 * t + 15], GM[:, 1, NOPE:QK],
                                                      ALU.mult, ALU.mult))
                    link(dve.tensor_scalar(GQK[:, 0, :], GQK[:, 0, :], HD ** -0.5, None, ALU.mult))
                    link(dve.tensor_scalar(GM[:, 0, :], GM[:, 0, :], QK ** -0.5, None, ALU.mult))
                    for i in range(2):
                        x = PRJ[:, :, i * SWA:(i + 1) * SWA].rearrange("p t (h c) -> p t h c", c=HD)
                        r = r15[:, :, 6 * i:6 * i + 6].unsqueeze(3).to_broadcast([P, T, HEADS, HD])
                        g = GQK[:, i, :].unsqueeze(1).unsqueeze(1).to_broadcast([P, T, HEADS, HD])
                        link(dve.tensor_tensor(x, x, r, ALU.mult))
                        link(dve.tensor_tensor(x, x, g, ALU.mult))

                @block.tensor
                def _(pe):
                    pe.wait_ge(cn, 8)
                    for i in range(3):
                        for t in range(T):
                            last = pe.transpose(PS[:, i, t * P:(t + 1) * P],
                                                PRJ[:, t, CQ0 + i * P:CQ0 + (i + 1) * P], eye[:, :])
                        last.then_inc(tp, 1)
                    pe.wait_ge(w_in, 32)
                    pe.wait_ge(ev, 3)
                    for t in range(T):
                        rows = slice(t * P, (t + 1) * P)
                        if t:
                            pe.wait_ge(mev, 4 * t)
                        for n in range(2):
                            for k in range(2):
                                last = pe.matmul(PS[:, 4 + n, 0:288], CT[:, k, rows], WUQ[:, k, n * 288:(n + 1) * 288],
                                                 start=(k == 0), stop=(k == 1))
                            last.then_inc(mm, 1)
                        for n in range(2):
                            pe.matmul(PS[:, 6 + n, 0:384], CT[:, 2, rows], WUKV[:, n * 384:(n + 1) * 384],
                                      start=True, stop=True).then_inc(mm, 1)

        with nc.Block() as block:
            @block.scalar
            def _(act):
                act.activation(SQ[:, 0:T * HEADS * QK], QM[:, :, :, :].rearrange("p t h c -> p (t h c)"),
                               ACT.Square).then_inc(sq3, 1)
                act.activation(SQ[:, 2304:2304 + T * HEADS * NOPE].rearrange("p (t h c) -> p (t h) c", h=HEADS, c=NOPE),
                               KV[:, :, :, 0:NOPE].rearrange("p t h c -> p (t h) c"), ACT.Square).then_inc(sq4, 1)

            @block.vector
            def _(dve):
                link.eng = dve
                n = T * HEADS
                q2 = SQ[:, 0:n * QK].rearrange("p (m c) -> p m c", c=QK)
                k2 = SQ[:, 2304:2304 + n * NOPE].rearrange("p (m c) -> p m c", c=NOPE)
                dve.wait_ge(sq3, 1)
                link(dve.tensor_reduce(V0[:, 0:n], q2[:, :, 0:NOPE], AX.X, ALU.add))
                link(dve.tensor_reduce(V0[:, n:2 * n], q2[:, :, NOPE:QK], AX.X, ALU.add))
                dve.wait_ge(sq4, 1)
                link(dve.tensor_reduce(V0[:, 2 * n:3 * n], k2, AX.X, ALU.add))
                for i, m in enumerate((NOPE, ROPE, NOPE)):
                    link(dve.tensor_scalar(V0[:, i * n:(i + 1) * n], V0[:, i * n:(i + 1) * n], 1.0 / m, EPS,
                                           ALU.mult, ALU.add))
                rsqrt(link, 3 * n)
                qm = QM[:, :, :, :].rearrange("p t h c -> p (t h) c")
                kc = KC[:, :, :, :].rearrange("p t h c -> p (t h) c")
                kv = KV[:, :, :, 0:NOPE].rearrange("p t h c -> p (t h) c")
                for x, y, w, r, g in ((qm[:, :, 0:NOPE], qm[:, :, 0:NOPE], NOPE, 0, GM[:, 0, 0:NOPE]),
                                      (qm[:, :, NOPE:QK], qm[:, :, NOPE:QK], ROPE, 1, GM[:, 0, NOPE:QK]),
                                      (kv, kc[:, :, 0:NOPE], NOPE, 2, GM[:, 1, 0:NOPE])):
                    rb = RS[:, r * n:(r + 1) * n].unsqueeze(2).to_broadcast([P, n, w])
                    link(dve.tensor_tensor(y, x, rb, ALU.mult))
                    link(dve.tensor_tensor(y, y, g.unsqueeze(1).to_broadcast([P, n, w]), ALU.mult))
                half = ROPE // 2
                for x, y, h in ((QM[:, :, :, NOPE:QK], QM[:, :, :, NOPE:QK], HEADS),
                                (PRJ[:, :, KR0:COLS].unsqueeze(2), None, 1)):
                    m = T * h * half
                    tmp = [SQ[:, i * m:(i + 1) * m].rearrange("p (t h c) -> p t h c", t=T, h=h) for i in range(4)]
                    cb = cosT[:, :, :].unsqueeze(2).to_broadcast([P, T, h, half])
                    sb_ = sinT[:, :, :].unsqueeze(2).to_broadcast([P, T, h, half])
                    x1, x2 = x[:, :, :, 0:half], x[:, :, :, half:ROPE]
                    link(dve.tensor_tensor(tmp[0], x1, cb, ALU.mult))
                    link(dve.tensor_tensor(tmp[1], x2, sb_, ALU.mult))
                    link(dve.tensor_tensor(tmp[2], x1, sb_, ALU.mult))
                    link(dve.tensor_tensor(tmp[3], x2, cb, ALU.mult))
                    if y is None:
                        y = PRJ[:, :, KR0:COLS].unsqueeze(2)
                    link(dve.tensor_tensor(y[:, :, :, 0:half], tmp[0], tmp[1], ALU.subtract))
                    link(dve.tensor_tensor(y[:, :, :, half:ROPE], tmp[2], tmp[3], ALU.add))
                link(dve.tensor_copy(KC[:, :, :, NOPE:QK],
                                     PRJ[:, :, KR0:COLS].unsqueeze(2).to_broadcast([P, T, HEADS, ROPE])))

        QT = sb("QT", [QK, 2 * HEADS, S])
        KT = sb("KT", [QK, 2 * HEADS, S])
        htp, hev_a, hev_d = sem_of("at_htp"), sem_of("at_hev_a"), sem_of("at_hev_d")
        lg, lmax, pexp, ptp, pev, omm, odone = (sem_of(f"at_{s}") for s in (
            "logits", "max", "exp", "ptp", "pev", "omm", "odone"))

        def head_source(i):
            h, isk = i // 2, i % 2
            dst = (KT if isk else QT)
            if h < HEADS:
                return dst[0:HD, h, :], lambda t: PRJ[:, t, isk * SWA + h * HD:isk * SWA + (h + 1) * HD], HD
            return dst[:, h, :], lambda t: (KC if isk else QM)[:, t, h - HEADS, :], QK

        pairs = [(h, t) for h in range(2 * HEADS) for t in range(T)]
        with nc.Block() as block:
            @block.tensor
            def _(pe):
                for i in range(4 * HEADS):
                    dst, src, w = head_source(i)
                    if i >= 4:
                        pe.wait_ge((hev_a, hev_d)[i % 2], (i - 4) // 2 + 1)
                    for t in range(T):
                        last = pe.transpose(PS[0:w, i % 4, t * P:(t + 1) * P], src(t), eye[:, :])
                    last.then_inc(htp, 1)
                pe.wait_ge(hev_a, 2 * HEADS)
                pe.wait_ge(hev_d, 2 * HEADS)

                def logits(i):
                    h, t = pairs[i]
                    w = HD if h < HEADS else QK
                    n = (t + 1) * P
                    if i >= 2:
                        pe.wait_ge(lmax, i - 1)
                    pe.matmul(PS[:, i % 2, 0:n], QT[0:w, h, t * P:(t + 1) * P], KT[0:w, h, 0:n],
                              start=True, stop=True).then_inc(lg, 1)

                def weigh(i):
                    h, t = pairs[i]
                    pe.wait_ge(pexp, i + 1)
                    if i >= 2:
                        pe.wait_ge(pev, i - 1)
                    for k in range(t + 1):
                        last = pe.transpose(PS[:, 2 + i % 2, k * P:(k + 1) * P],
                                            HT[:, i % 2, k * P:(k + 1) * P], eye[:, :])
                    last.then_inc(ptp, 1)

                def mix(i):
                    h, t = pairs[i]
                    pe.wait_ge(pev, i + 1)
                    if i >= 2:
                        pe.wait_ge(odone, i - 1)
                    for k in range(t + 1):
                        v = (PRJ[:, k, 2 * SWA + h * HD:2 * SWA + (h + 1) * HD] if h < HEADS
                             else KV[:, k, h - HEADS, NOPE:NOPE + HD])
                        last = pe.matmul(PS[:, 4 + i % 2, 0:HD], HT[:, 2 + i % 2, k * P:(k + 1) * P], v,
                                         start=(k == 0), stop=(k == t))
                    last.then_inc(omm, 1)

                N = len(pairs)
                for i in range(N + 2):
                    if i < N:
                        logits(i)
                    if 1 <= i <= N:
                        weigh(i - 1)
                    if i >= 2:
                        mix(i - 2)

            @block.scalar
            def _(act):
                for i in range(0, 4 * HEADS, 2):
                    dst, _, w = head_source(i)
                    act.wait_ge(htp, i + 1)
                    act.activation(dst, PS[0:w, i % 4, :], ACT.Copy).then_inc(hev_a, 1)

                def evac(i):
                    n = (pairs[i][1] + 1) * P
                    act.wait_ge(ptp, i + 1)
                    if i >= 2:
                        act.wait_ge(omm, i - 1)
                    act.activation(HT[:, 2 + i % 2, 0:n], PS[:, 2 + i % 2, 0:n], ACT.Copy).then_inc(pev, 1)

                for i, (h, t) in enumerate(pairs):
                    n = (t + 1) * P
                    act.wait_ge(lmax, i + 1)
                    act.activation(HT[:, i % 2, 0:n], HT[:, i % 2, 0:n], ACT.Exp, bias=V0[:, 2 * (i % 2):2 * (i % 2) + 1],
                                   accum_out=RS[:, i % 4:i % 4 + 1]).then_inc(pexp, 1)
                    if i >= 1:
                        evac(i - 1)
                evac(len(pairs) - 1)

            @block.vector
            def _(dve):
                link.eng = dve
                for i in range(1, 4 * HEADS, 2):
                    dst, _, w = head_source(i)
                    dve.wait_ge(htp, i + 1)
                    link(dve.tensor_copy(dst, PS[0:w, i % 4, :]), hev_d)

                def finish(i):
                    h, t = pairs[i]
                    c = 8 + i % 2
                    dve.wait_ge(pexp, i + 1)
                    link(dve.reciprocal(V0[:, c:c + 1], RS[:, i % 4:i % 4 + 1]))
                    dve.wait_ge(omm, i + 1)
                    y0 = h * HD if h < HEADS else SWA + S5C + (h - HEADS) * HD
                    link(dve.tensor_scalar(H[:, t, y0:y0 + HD], PS[:, 4 + i % 2, 0:HD], V0[:, c:c + 1], None,
                                           ALU.mult), odone)

                for i, (h, t) in enumerate(pairs):
                    n = (t + 1) * P
                    b = min(h, HEADS)
                    c = 2 * (i % 2)
                    dve.wait_ge(lg, i + 1)
                    if i >= 2:
                        dve.wait_ge(ptp, i - 1)
                    link(dve.tensor_tensor_reduce(HT[:, i % 2, 0:n], PS[:, i % 2, 0:n], BM[:, b, S - n:S], 1.0, LOWEST,
                                                  ALU.add, ALU.max, V0[:, c + 1:c + 2]))
                    link(dve.tensor_scalar(V0[:, c:c + 1], V0[:, c + 1:c + 2], -1.0, None, ALU.mult), lmax)
                    if i >= 2:
                        finish(i - 2)
                finish(len(pairs) - 2)
                finish(len(pairs) - 1)


def peer(nc, a, layer, link, sem_of, PS, X, MOD, H, HT, eye, lst, loff,
         ring_in, ring_free, ring_taken, staged, act_ready, gated, out_step, peer_step, peer_exp):
    with ExitStack() as st:
        def sb(name, shape, dt=F32):
            return st.enter_context(nc.sbuf_tensor(name, shape, dt))

        IDX = sb("IDX", [P, T, SLOTS], U32)
        GATE = sb("GATE", [P, T, SLOTS])
        with ExitStack() as route:
            def rb(name, shape, dt=F32):
                return route.enter_context(nc.sbuf_tensor(name, shape, dt))

            QP = rb("QP", [P, 2 * PH, S])
            SKT = rb("SKT", [P, 2 * PH, P])
            wq_in = [sem_of(f"wq_in{i}") for i in range(2)]
            sk_in, sk_tp, sk_ev, q_mm = (sem_of(f"r_{s}") for s in ("sk_in", "sk_tp", "sk_ev", "q_mm"))
            q_ev = [sem_of("r_q_ev_act"), sem_of("r_q_ev_dve")]
            with ExitStack() as load:
                WQ = load.enter_context(nc.sbuf_tensor("WQ", [P, 2, KD, 512], F32))
                SK = load.enter_context(nc.sbuf_tensor("SK", [P, 2 * PH, P], F32))
                with nc.Block() as block:
                    @block.sync
                    def _(sp):
                        keys = a["peer_subkeys"][layer].rearrange("h j k d -> k (h j) d")
                        for i in range(2 * PH):
                            sp.dma_start(SK[:, i, :], keys[:, i, :]).then_inc(sk_in, 16)
                        for n in range(4):
                            if n >= 2:
                                sp.wait_ge(q_mm, 4 * (n - 1))
                            sp.dma_start(WQ[:, n % 2, :, :], a["peer_wq"][layer, :, n * 512:(n + 1) * 512]
                                         .rearrange("(k p) n -> p k n", p=P)).then_inc(wq_in[n % 2], 16)

                    @block.tensor
                    def _(pe):
                        pe.wait_ge(sk_in, 16 * 2 * PH)
                        for g in range(4):
                            for i in range(4):
                                last = pe.transpose(PS[:, 4 + g, i * P:(i + 1) * P], SK[:, 4 * g + i, :], eye[:, :])
                            last.then_inc(sk_tp, 1)
                        for j in range(16):
                            pe.wait_ge(wq_in[j // 4 % 2], 16 * (j // 8 + 1))
                            if j >= 4:
                                pe.wait_ge(q_ev[j % 2], (j - 4) // 2 + 1)
                            for k in range(KD):
                                last = pe.matmul(PS[:, j % 4, :], WQ[:, j // 4 % 2, k, (j % 4) * P:(j % 4 + 1) * P],
                                                 HT[:, k, :], start=(k == 0), stop=(k == KD - 1))
                            last.then_inc(q_mm, 1)

                    @block.scalar
                    def _(act):
                        for g in range(4):
                            act.wait_ge(sk_tp, g + 1)
                            act.activation(SKT[:, 4 * g:4 * g + 4, :].rearrange("p a b -> p (a b)"), PS[:, 4 + g, :],
                                           ACT.Copy).then_inc(sk_ev, 1)
                        for j in range(0, 16, 2):
                            act.wait_ge(q_mm, j + 1)
                            act.activation(QP[:, j, :], PS[:, j % 4, :], ACT.Copy).then_inc(q_ev[0], 1)

                    @block.vector
                    def _(dve):
                        for j in range(1, 16, 2):
                            dve.wait_ge(q_mm, j + 1)
                            dve.tensor_copy(QP[:, j, :], PS[:, j % 4, :]).then_inc(q_ev[1], 1)

            SC = rb("SC", [P, 2 * PH, P])
            T1 = rb("T1", [P, 2 * PH, TOPK])
            I1 = rb("I1", [P, 2 * PH, TOPK], U32)
            I1f = rb("I1f", [P, 2 * PH, TOPK])
            CA = rb("CA", [P, PH, TOPK * TOPK])
            B1 = rb("B1", [P, PH, TOPK])
            BC = rb("BC", [P, PH, TOPK], U32)
            B2 = rb("B2", [P, 2, SLOTS], U32)
            B2f = rb("B2f", [P, 2, SLOTS])
            EQ = rb("EQ", [P, SLOTS, TOPK])
            EX = rb("EX", [P, 2, SLOTS])
            SU = rb("SU", [P, PH])
            s_mm, s_ev, g_in, g_exp = (sem_of(f"r_{s}") for s in ("s_mm", "s_ev", "g_in", "g_exp"))
            s_free = sem_of("r_s_free")
            with nc.Block() as block:
                @block.tensor
                def _(pe):
                    for t in range(T):
                        if t:
                            pe.wait_ge(s_ev, t)
                        for j in range(16):
                            last = pe.matmul(PS[:, j // 4, (j % 4) * P:(j % 4 + 1) * P], QP[:, j, t * P:(t + 1) * P],
                                             SKT[:, j, :], start=True, stop=True)
                        last.then_inc(s_mm, 1)

                @block.scalar
                def _(act):
                    for t in range(T):
                        act.wait_ge(s_mm, t + 1)
                        if t:
                            act.wait_ge(s_free, t)
                        act.activation(SC[:, :, :].rearrange("p (b j) k -> p b (j k)", b=4), PS[:, 0:4, :],
                                       ACT.Copy).then_inc(s_ev, 1)
                        act.wait_ge(g_in, t + 1)
                        act.activation(GATE[:, t, :], GATE[:, t, :], ACT.Exp).then_inc(g_exp, 1)

                @block.vector
                def _(dve):
                    link.eng = dve

                    def top16(values, tops, places):
                        link(dve.max(tops[:, 0:8], values))
                        link(dve.max_index(places[:, 0:8], tops[:, 0:8], values))
                        link(dve.match_replace(values, tops[:, 0:8], values, LOWEST))
                        link(dve.max(tops[:, 8:16], values))
                        link(dve.max_index(places[:, 8:16], tops[:, 8:16], values))

                    for t in range(T):
                        dve.wait_ge(s_ev, t + 1)
                        for j in range(2 * PH):
                            top16(SC[:, j, :], T1[:, j, :], I1[:, j, :])
                        dve.sem_inc(s_free, 1)
                        t4 = T1[:, :, :].rearrange("p (h j) k -> p h j k", j=2)
                        link(dve.tensor_tensor(CA[:, :, :].rearrange("p h (x y) -> p h x y", x=TOPK),
                                               t4[:, :, 0, :].unsqueeze(3).to_broadcast([P, PH, TOPK, TOPK]),
                                               t4[:, :, 1, :].unsqueeze(2).to_broadcast([P, PH, TOPK, TOPK]), ALU.add))
                        for h in range(PH):
                            top16(CA[:, h, :], B1[:, h, :], BC[:, h, :])
                        gate = GATE[:, t, :].rearrange("p (h s) -> p h s", h=PH)
                        link(dve.tensor_tensor(gate, B1[:, :, :], B1[:, :, 0:1].to_broadcast([P, PH, TOPK]),
                                               ALU.subtract), g_in)
                        bc = BC[:, :, :].rearrange("p h s -> p (h s)")
                        link(dve.tensor_scalar(B2[:, 0, :], bc, 4, None, ALU.logical_shift_right))
                        link(dve.tensor_scalar(B2[:, 1, :], bc, 15, None, ALU.bitwise_and))
                        link(dve.tensor_copy(B2f[:, :, :], B2[:, :, :]))
                        link(dve.tensor_copy(I1f[:, :, :], I1[:, :, :]))
                        i4 = I1f[:, :, :].rearrange("p (h j) k -> p h j k", j=2)
                        for i in range(2):
                            eq4 = EQ[:, :, :].rearrange("p (h s) k -> p h s k", h=PH)
                            link(dve.tensor_tensor(EQ[:, :, :], B2f[:, i, :].unsqueeze(2).to_broadcast([P, SLOTS, TOPK]),
                                                   lst[:, :].unsqueeze(1).to_broadcast([P, SLOTS, TOPK]),
                                                   ALU.is_equal))
                            link(dve.tensor_tensor(eq4, eq4, i4[:, :, i, :].unsqueeze(2)
                                                   .to_broadcast([P, PH, TOPK, TOPK]), ALU.mult))
                            link(dve.tensor_reduce(EX[:, i, :], EQ[:, :, :], AX.X, ALU.add))
                        link(dve.scalar_tensor_tensor(EX[:, 0, :], EX[:, 0, :], float(KEYS), EX[:, 1, :],
                                                      ALU.mult, ALU.add))
                        link(dve.tensor_scalar(IDX[:, t, :], EX[:, 0, :], loff[:, 0:1], None, ALU.add))
                        dve.wait_ge(g_exp, t + 1)
                        link(dve.tensor_reduce(SU[:, :], gate, AX.X, ALU.add))
                        link(dve.reciprocal(SU[:, :], SU[:, :]))
                        link(dve.tensor_tensor(gate, gate, SU[:, :].unsqueeze(2).to_broadcast([P, PH, TOPK]),
                                               ALU.mult))
                    link(dve.tensor_scalar(loff[:, :], loff[:, :], float(EXPERTS), None, ALU.add))

        rows = sb("rows_ring", [P, RING, D])
        nxt = sb("idx_next", [P, 2, RING], U32)
        W = sb("W", [P, 2, SLOTS])
        ACC = sb("ACC", [P, D])
        tabs = [a["peer_u"].rearrange("l e d -> (l e) d"), a["peer_v"].rearrange("l e d -> (l e) d")]
        PASS = SLOTS
        STEP = 2 * RING
        with nc.Block() as block:
            @block.scalar
            def _(act):
                with act.Fori(0, T) as t:
                    def stage(side, g, j):
                        act.wait_ge(ring_free, ((layer * T + t) * 2 + side) * PASS + g * STEP + j * RING + 1)
                        act.activation(nxt[:, j, :], IDX[:, t, bass.ds(g * STEP + j * RING, RING)], ACT.Copy)\
                            .then_inc(staged, 1)

                    with act.Fori(0, PASS // STEP) as g:
                        stage(0, g, 0)
                        stage(0, g, 1)
                    stage(1, 0, 0)
                    stage(1, 0, 1)
                    act.wait_ge(act_ready, layer * T + t + 1)
                    act.activation(W[:, 1, :], W[:, 1, :], ACT.Exp).then_inc(peer_exp, 1)
                    with act.Fori(1, PASS // STEP) as g:
                        stage(1, g, 0)
                        stage(1, g, 1)

            @block.gpsimd
            def _(pool):
                with pool.Fori(0, T) as t:
                    for side in range(2):
                        with pool.Fori(0, PASS // STEP) as g:
                            for j in range(2):
                                n = ((layer * T + t) * 2 + side) * PASS + g * STEP + j * RING
                                pool.wait_ge(staged, ((layer * T + t) * 2 + side) * (PASS // RING) + g * 2 + j + 1)
                                for b in range(RING):
                                    pool.wait_ge(ring_free, n + b + 2)
                                    pool.sem_inc(ring_taken, 1)
                                    pool.indirect_dma_start(
                                        out=rows[:, b, :], out_offset=None, in_=tabs[side],
                                        in_offset=bass.IndirectOffsetOnAxis(ap=nxt[:, j, b:b + 1], axis=0))\
                                        .then_inc(ring_in[b], 16)

            @block.vector
            def _(dve):
                pstep = 0
                with dve.Fori(0, T) as t:
                    with dve.Fori(0, PASS // RING) as g:
                        for b in range(RING):
                            dve.wait_ge(ring_in[b], 16 * ((((layer * T + t) * 2) * (PASS // RING)) + g + 1))
                            dve.scalar_tensor_tensor(rows[:, b, :], rows[:, b, :], 1.0, H[:, t, :], ALU.mult, ALU.mult,
                                                     accum_out=W[:, 0, bass.ds(g * RING + b, 1)]).then_inc(ring_free, 1)
                    dve.wait_ge(ring_free, CREDIT + ((layer * T + t) * 2 + 1) * PASS)
                    base = (layer * T + t) * 8

                    def plink(ins):
                        nonlocal pstep
                        pstep += 1
                        ins.then_inc(peer_step, 1)
                        dve.wait_ge(peer_step, base + pstep)

                    y, g_ = W[:, 0, :], W[:, 1, :]
                    gelu_terms(plink, dve, y, g_)
                    dve.sem_inc(act_ready, 1)
                    plink(dve.memset(ACC[:, :], 0.0))
                    plink(dve.tensor_tensor(y, y, GATE[:, t, :], ALU.mult))
                    dve.wait_ge(peer_exp, layer * T + t + 1)
                    plink(dve.tensor_scalar(g_, g_, 1.0, None, ALU.add))
                    plink(dve.reciprocal(g_, g_))
                    dve.tensor_tensor(y, y, g_, ALU.mult).then_inc(gated, 1)
                    with dve.Fori(0, PASS // RING) as g:
                        dve.wait_ge(gated, layer * T + t + 1)
                        for b in range(RING):
                            n = ((layer * T + t) * 2 + 1) * PASS + g * RING + b
                            dve.wait_ge(ring_in[b], 16 * ((((layer * T + t) * 2 + 1) * (PASS // RING)) + g + 1))
                            dve.wait_ge(ring_free, CREDIT + n)
                            dve.scalar_tensor_tensor(ACC[:, :], rows[:, b, :], W[:, 0, bass.ds(g * RING + b, 1)],
                                                     ACC[:, :], ALU.mult, ALU.add).then_inc(ring_free, 1)
                    dve.wait_ge(ring_free, CREDIT + ((layer * T + t) * 2 + 2) * PASS)
                    dve.tensor_tensor(ACC[:, :], ACC[:, :], MOD[:, 5, :], ALU.mult).then_inc(out_step, 1)
                    dve.wait_ge(out_step, 2 * (layer * T + t) + 1)
                    dve.tensor_tensor(X[:, t, :], X[:, t, :], ACC[:, :], ALU.add).then_inc(out_step, 1)
                    dve.wait_ge(out_step, 2 * (layer * T + t) + 2)


def build(nc, a, out):
    outer = ExitStack()
    with outer:
        def tensors(stack):
            def sb(name, shape, dt=F32):
                return stack.enter_context(nc.sbuf_tensor(name, shape, dt))
            return sb

        sems = []

        def sem(name, keep=False):
            s = outer.enter_context(nc.semaphore(name))
            if not keep:
                sems.append(s)
            return s

        sb = tensors(outer)
        X = sb("X", [P, T, D])
        MOD = sb("MOD", [P, 6, D])
        H = sb("H", [P, T, D])
        HT = sb("HT", [P, KD, S])
        BM = sb("BM", [P, HEADS + 1, S])
        eye = sb("eye", [P, P])
        cosT = sb("cosT", [P, T, 16])
        sinT = sb("sinT", [P, T, 16])
        blk = sb("blk", [P, SJ, 8])
        rowpar = sb("rowpar", [P, P])
        means = sb("means", [P, 16])
        lst = sb("lst", [P, TOPK])
        CB = sb("CB", [P, KD, P])
        loff = sb("loff", [P, 1])
        RS = sb("RS", [P, 96])
        V0 = sb("V0", [P, 96])
        NT = sb("NT", [P, 2, 96])
        PS = outer.enter_context(nc.psum_tensor("PS", [P, 8, 512], F32))
        toep = nc.dram_tensor("toep", (HEADS + 1, TOEP), F32, kind="Internal").ap()

        dve_step = sem("dve_step")
        act_step = sem("act_step")
        pool_step = sem("pool_step")
        dve_layer = sem("dve_layer", keep=True)
        act_layer = sem("act_layer", keep=True)

        def rsqrt(link, n, terms=3):
            v, y, t = V0[:, 0:n], RS[:, 0:n], NT[:, 0, 0:n]
            dve = nc.vector
            link(dve.tensor_scalar(t.bitcast(I32), v.bitcast(I32), 1, None, ALU.logical_shift_right))
            link(dve.tensor_scalar(y.bitcast(I32), t.bitcast(I32), -1.0, float(0x5F3759DF), ALU.mult, ALU.add))
            for _ in range(terms):
                link(dve.tensor_tensor(t, y, y, ALU.mult))
                link(dve.tensor_tensor(t, t, v, ALU.mult))
                link(dve.tensor_scalar(t, t, -0.5, 1.5, ALU.mult, ALU.add))
                link(dve.tensor_tensor(y, y, t, ALU.mult))

        with ExitStack() as st:
            sb = tensors(st)
            rows = sb("rows", [BUCKETS + 2, TOEP])
            sel = sb("sel", [BUCKETS + 2, HEADS + 1])
            flip = sb("flip", [P, P])
            ccol = sb("ccol", [P, 3, KD])
            wr = sb("wr", [HEADS + 1, TOEP])
            BMr = sb("BMr", [P, HEADS + 1, S])
            loads = sem("once_loads")
            sel_in = sem("sel_in")
            rel_in = sem("rel_in")
            bias_rows = sem("bias_rows")
            bias_copied = sem("bias_copied")
            bias_stored = sem("bias_stored")
            bias_back = sem("bias_back")
            bias_flipped = sem("bias_flipped")
            exp_c = sem("exp_c")
            n_loads = 11
            with nc.Block() as block:
                @block.sync
                def _(sp):
                    sp.dma_start(sel[:, :], a["c_sel"]).then_inc(sel_in, 16)
                    sp.dma_start(ccol[:, 0, :], a["c"].rearrange("a (k p) -> p (a k)", p=P),
                                 allow_slow_non_contiguous=True).then_inc(loads, 16)
                    sp.dma_start(rows[:, :], a["c_rows"]).then_inc(loads, 16)
                    sp.dma_start(flip[:, :], a["c_flip"]).then_inc(loads, 16)
                    sp.dma_start(eye[:, :], a["c_eye"]).then_inc(loads, 16)
                    sp.dma_start(cosT[:, :, :], a["c_cos"].rearrange("(t p) f -> p t f", p=P)).then_inc(loads, 16)
                    sp.dma_start(sinT[:, :, :], a["c_sin"].rearrange("(t p) f -> p t f", p=P)).then_inc(loads, 16)
                    sp.dma_start(blk[:, :, :], a["c_blk"].rearrange("p (j b) -> p j b", b=8)).then_inc(loads, 16)
                    sp.dma_start(rowpar[:, :], a["c_rowpar"]).then_inc(loads, 16)
                    sp.dma_start(means[:, :], a["c_means"]).then_inc(loads, 16)
                    sp.dma_start(lst[:, :], a["c_list"]).then_inc(loads, 16)
                    sp.dma_start(X[:, :, :], a["x"].rearrange("a (t p) d -> p (a t) d", p=P)).then_inc(loads, 16)
                    sp.wait_ge(sel_in, 16)
                    sp.dma_start(sel[0:BUCKETS, 0:HEADS], a["rel_bias"].rearrange("h b -> b h"),
                                 allow_slow_non_contiguous=True).then_inc(rel_in, 16)
                    sp.wait_ge(bias_copied, 2)
                    sp.dma_start(toep, wr[:, :]).then_inc(bias_stored, 16)
                    sp.wait_ge(bias_stored, 16)
                    for h in range(HEADS + 1):
                        shifted = bass.AP(toep.tensor, h * TOEP, [[1, P], [1, S]])
                        sp.dma_start(BMr[:, h, :], shifted).then_inc(bias_back, 16)
                    sp.wait_ge(bias_back, 16 * (HEADS + 1))

                @block.tensor
                def _(pe):
                    pe.wait_ge(loads, 16 * n_loads)
                    pe.wait_ge(rel_in, 16)
                    for half in range(2):
                        pe.matmul(PS[0:HEADS + 1, half, 0:320], sel[:, :], rows[:, half * 320:half * 320 + 320],
                                  start=True, stop=True).then_inc(bias_rows, 1)
                    pe.wait_ge(bias_back, 16 * (HEADS + 1))
                    for h in range(HEADS + 1):
                        pe.matmul(PS[:, 1 + h, :], flip[:, :], BMr[:, h, :], start=True, stop=True)\
                            .then_inc(bias_flipped, 1)

                @block.scalar
                def _(act):
                    act.wait_ge(loads, 16 * n_loads)
                    act.activation(ccol[:, 1, :], ccol[:, 0, :], ACT.Exp, scale=-1.0).then_inc(exp_c, 1)

                @block.vector
                def _(dve):
                    link = Link(dve, dve_step)
                    for half in range(2):
                        dve.wait_ge(bias_rows, half + 1)
                        dve.tensor_copy(wr[:, half * 320:half * 320 + 320], PS[0:HEADS + 1, half, 0:320])\
                            .then_inc(bias_copied, 1)
                    dve.wait_ge(exp_c, 1)
                    link(dve.tensor_scalar(ccol[:, 1, :], ccol[:, 1, :], 1.0, None, ALU.add))
                    link(dve.reciprocal(ccol[:, 2, :], ccol[:, 1, :]))
                    link(dve.tensor_tensor(ccol[:, 0, :], ccol[:, 0, :], ccol[:, 2, :], ALU.mult))
                    link(dve.tensor_copy(CB[:, :, :], ccol[:, 0, :].unsqueeze(2).to_broadcast([P, KD, P])))
                    link(dve.memset(loff[:, :], 0.0))
                    for h in range(HEADS + 1):
                        dve.wait_ge(bias_flipped, h + 1)
                        link(dve.tensor_copy(BM[:, h, :], PS[:, 1 + h, :]))

        def clear_all():
            with nc.Block() as block:
                @block.vector
                def _(dve):
                    for s in sems:
                        dve.sem_clear(s)

        clear_all()

        ring_in = [sem(f"ring_in{b}", keep=True) for b in range(RING)]
        ring_free = sem("ring_free", keep=True)
        ring_taken = sem("ring_taken", keep=True)
        staged = sem("idx_staged", keep=True)
        act_ready = sem("act_ready", keep=True)
        gated = sem("gated", keep=True)
        out_step = sem("out_step", keep=True)
        peer_step = sem("peer_step", keep=True)
        peer_exp = sem("peer_exp", keep=True)

        with nc.Block() as block:
            @block.vector
            def _(dve):
                dve.sem_inc(ring_free, CREDIT)

        wbuf_in = [sem(f"wbuf_in{i}") for i in range(2)]
        mod_mm = sem("mod_mm")
        mod_ev = sem("mod_ev")
        mod_loads = sem("mod_loads")

        names = {}

        def named(name):
            if name not in names:
                names[name] = sem(name)
            return names[name]

        def norm_block(which, scale, shift):
            ss, hs, tp, ev = (named(f"n{which}_{s}") for s in ("sumsq", "h", "tp", "ev"))
            with nc.Block() as block:
                @block.scalar
                def _(act):
                    for t in range(T):
                        act.activation(H[:, t, :], X[:, t, :], ACT.Square, accum_out=V0[:, t:t + 1]).then_inc(ss, 1)
                    for t in range(T):
                        act.wait_ge(tp, t + 1)
                        b = 2 * (t % 2)
                        act.activation(HT[:, :, t * P:(t + 1) * P],
                                       PS[:, b:b + 2, :].rearrange("p b (k c) -> p (b k) c", c=P),
                                       ACT.Copy).then_inc(ev, 1)

                @block.vector
                def _(dve):
                    link.eng = dve
                    dve.wait_ge(ss, T)
                    link(dve.tensor_scalar(V0[:, 0:T], V0[:, 0:T], 1.0 / D, EPS, ALU.mult, ALU.add))
                    rsqrt(link, T)
                    for t in range(T):
                        link(dve.scalar_tensor_tensor(H[:, t, :], X[:, t, :], RS[:, t:t + 1], MOD[:, scale, :],
                                                      ALU.mult, ALU.mult))
                        link(dve.tensor_tensor(H[:, t, :], H[:, t, :], MOD[:, shift, :], ALU.add), hs)

                @block.tensor
                def _(pe):
                    for t in range(T):
                        pe.wait_ge(hs, t + 1)
                        if t >= 2:
                            pe.wait_ge(ev, t - 1)
                        for k in range(KD):
                            last = pe.transpose(PS[:, 2 * (t % 2) + k // 4, (k % 4) * P:(k % 4 + 1) * P],
                                                H[:, t, k * P:(k + 1) * P], eye[:, :])
                        last.then_inc(tp, 1)

        with nc.Fori(0, DEPTH) as layer:
            link = Link(nc.vector, dve_step)
            with ExitStack() as st:
                sb = tensors(st)
                WA = sb("WA", [P, 2, KD, 512])
                GB = sb("GB", [P, 2, D])
                with nc.Block() as block:
                    @block.sync
                    def _(sp):
                        sp.dma_start(MOD[:, :, :].rearrange("p s d -> p (s d)"),
                                     a["b_ada"][layer, :].partition_broadcast(P)).then_inc(mod_loads, 16)
                        sp.dma_start(GB[:, 0, :], a["norm1_gain"][layer, :].partition_broadcast(P)).then_inc(mod_loads, 16)
                        sp.dma_start(GB[:, 1, :], a["norm2_gain"][layer, :].partition_broadcast(P)).then_inc(mod_loads, 16)
                        for n in range(12):
                            if n >= 2:
                                sp.wait_ge(mod_mm, n - 1)
                            sp.dma_start(WA[:, n % 2, :, :],
                                         a["w_ada"][layer, :, n * 512:(n + 1) * 512].rearrange("(k p) n -> p k n", p=P))\
                                .then_inc(wbuf_in[n % 2], 16)

                    @block.tensor
                    def _(pe):
                        for n in range(12):
                            pe.wait_ge(wbuf_in[n % 2], 16 * (n // 2 + 1))
                            if n >= 2:
                                pe.wait_ge(mod_ev, n - 1)
                            for k in range(KD):
                                last = pe.matmul(PS[:, n % 2, :], CB[:, k, :], WA[:, n % 2, k, :],
                                                 start=(k == 0), stop=(k == KD - 1))
                            last.then_inc(mod_mm, 1)

                    @block.vector
                    def _(dve):
                        link.eng = dve
                        dve.wait_ge(mod_loads, 48)
                        for n in range(12):
                            dve.wait_ge(mod_mm, n + 1)
                            m = MOD[:, n // 2, (n % 2) * 512:(n % 2 + 1) * 512]
                            link(dve.tensor_tensor(m, PS[:, n % 2, :], m, ALU.add), mod_ev)
                        for i, s in enumerate((1, 4)):
                            link(dve.scalar_tensor_tensor(MOD[:, s, :], MOD[:, s, :], 1.0, GB[:, i, :],
                                                          ALU.add, ALU.mult))

            norm_block(1, 1, 0)

            with ExitStack() as mix:
                sb = tensors(mix)
                PRJ = sb("PRJ", [P, T, COLS])
                wi_in = [named(f"wi_in{i}") for i in range(2)]
                pj_mm, pj_ev = named("pj_mm"), [named("pj_ev_act"), named("pj_ev_dve")]
                NCH = COLS // 4
                with ExitStack() as st:
                    WI = tensors(st)("WI", [P, 2, KD, NCH])
                    with nc.Block() as block:
                        @block.sync
                        def _(sp):
                            for n in range(4):
                                if n >= 2:
                                    sp.wait_ge(pj_mm, 4 * (n - 1))
                                sp.dma_start(WI[:, n % 2, :, :],
                                             a["w_in"][layer, :, n * NCH:(n + 1) * NCH]
                                             .rearrange("(k p) n -> p k n", p=P)).then_inc(wi_in[n % 2], 16)

                        @block.tensor
                        def _(pe):
                            for i in range(16):
                                n, t = i // 4, i % 4
                                pe.wait_ge(wi_in[n % 2], 16 * (n // 2 + 1))
                                if i >= 4:
                                    pe.wait_ge(pj_ev[i % 2], (i - 4) // 2 + 1)
                                for k in range(KD):
                                    last = pe.matmul(PS[:, i % 4, 0:NCH], HT[:, k, t * P:(t + 1) * P],
                                                     WI[:, n % 2, k, :], start=(k == 0), stop=(k == KD - 1))
                                last.then_inc(pj_mm, 1)

                        @block.scalar
                        def _(act):
                            for i in range(0, 16, 2):
                                n, t = i // 4, i % 4
                                act.wait_ge(pj_mm, i + 1)
                                act.activation(PRJ[:, t, n * NCH:(n + 1) * NCH], PS[:, i % 4, 0:NCH], ACT.Copy)\
                                    .then_inc(pj_ev[0], 1)

                        @block.vector
                        def _(dve):
                            for i in range(1, 16, 2):
                                n, t = i // 4, i % 4
                                dve.wait_ge(pj_mm, i + 1)
                                dve.tensor_copy(PRJ[:, t, n * NCH:(n + 1) * NCH], PS[:, i % 4, 0:NCH])\
                                    .then_inc(pj_ev[1], 1)

                s5_block(nc, a, layer, link, named, PS, PRJ, H, HT, eye, blk, rowpar)
                attention(nc, a, layer, link, named, PS, PRJ, H, HT, eye, means, BM, cosT, sinT, RS, V0, rsqrt)

            with ExitStack() as st:
                sb = tensors(st)
                WO = sb("WO", [P, KD, D])
                MG = sb("MG", [P, D])
                TMP = sb("TMP", [P, 2, 512])
                wo_in, ss, yn, tp, ev, mm, res = (named(f"out_{s}") for s in
                                                  ("w", "sumsq", "y", "tp", "ev", "mm", "res"))
                parts = [(0, SWA), (SWA, SWA + S5C), (SWA + S5C, D)]
                with nc.Block() as block:
                    @block.sync
                    def _(sp):
                        sp.dma_start(MG[:, :], a["mix_gain"][layer, :].partition_broadcast(P)).then_inc(wo_in, 16)
                        sp.dma_start(WO[:, :, :], a["w_out"][layer].rearrange("(k p) n -> p k n", p=P))\
                            .then_inc(wo_in, 16)

                    @block.scalar
                    def _(act):
                        for t in range(T):
                            for i, (lo, hi) in enumerate(parts):
                                act.activation(HT[:, 2 * t:2 * t + 2, :].rearrange("p a b -> p (a b)")[:, lo:hi],
                                               H[:, t, lo:hi], ACT.Square,
                                               accum_out=V0[:, 4 * i + t:4 * i + t + 1]).then_inc(ss, 1)
                        for t in range(T):
                            act.wait_ge(tp, t + 1)
                            b = 2 * (t % 2)
                            act.activation(HT[:, :, t * P:(t + 1) * P],
                                           PS[:, b:b + 2, :].rearrange("p b (k c) -> p (b k) c", c=P),
                                           ACT.Copy).then_inc(ev, 1)

                    @block.vector
                    def _(dve):
                        link.eng = dve
                        dve.wait_ge(ss, 3 * T)
                        for i, (lo, hi) in enumerate(parts):
                            link(dve.tensor_scalar(V0[:, 4 * i:4 * i + 4], V0[:, 4 * i:4 * i + 4],
                                                   1.0 / (hi - lo), EPS, ALU.mult, ALU.add))
                        rsqrt(link, 12)
                        dve.wait_ge(wo_in, 32)
                        for t in range(T):
                            for i, (lo, hi) in enumerate(parts):
                                link(dve.scalar_tensor_tensor(H[:, t, lo:hi], H[:, t, lo:hi],
                                                              RS[:, 4 * i + t:4 * i + t + 1], MG[:, lo:hi],
                                                              ALU.mult, ALU.mult), yn)
                        for i in range(8):
                            n, t = i // 4, i % 4
                            cols = slice(n * 512, (n + 1) * 512)
                            dve.wait_ge(mm, i + 1)
                            link(dve.tensor_tensor(TMP[:, i % 2, :], PS[:, 4 + i % 4, :], MOD[:, 2, cols],
                                                   ALU.mult), res)
                            link(dve.tensor_tensor(X[:, t, cols], X[:, t, cols], TMP[:, i % 2, :], ALU.add))

                    @block.tensor
                    def _(pe):
                        for t in range(T):
                            pe.wait_ge(yn, 3 * (t + 1))
                            if t >= 2:
                                pe.wait_ge(ev, t - 1)
                            for k in range(KD):
                                last = pe.transpose(PS[:, 2 * (t % 2) + k // 4, (k % 4) * P:(k % 4 + 1) * P],
                                                    H[:, t, k * P:(k + 1) * P], eye[:, :])
                            last.then_inc(tp, 1)
                        pe.wait_ge(wo_in, 32)
                        pe.wait_ge(ev, T)
                        for i in range(8):
                            n, t = i // 4, i % 4
                            if i >= 4:
                                pe.wait_ge(res, i - 3)
                            for k in range(KD):
                                last = pe.matmul(PS[:, 4 + i % 4, :], HT[:, k, t * P:(t + 1) * P],
                                                 WO[:, k, n * 512:(n + 1) * 512], start=(k == 0), stop=(k == KD - 1))
                            last.then_inc(mm, 1)

            norm_block(2, 4, 3)
            peer(nc, a, layer, link, named, PS, X, MOD, H, HT, eye, lst, loff,
                 ring_in, ring_free, ring_taken, staged, act_ready, gated, out_step, peer_step, peer_exp)
            clear_all()

        stored = sem("stored")
        with nc.Block() as block:
            @block.sync
            def _(sp):
                sp.dma_start(out.rearrange("a (t p) d -> p (a t) d", p=P), X[:, :, :]).then_inc(stored, 16)
                sp.wait_ge(stored, 16)


INPUTS = ["x", "c", "w_in", "w_out", "mix_gain", "norm1_gain", "norm2_gain", "w_ada", "b_ada", "rel_bias",
          "swa_q_gain", "swa_k_gain", "mla_q_lora_gain", "mla_kv_lora_gain", "w_uq", "w_ukv", "mla_q_gain",
          "mla_k_gain", "s5_a_re", "s5_a_im", "s5_b_re", "s5_b_im", "s5_c_re", "s5_c_im", "s5_d", "s5_log_dt",
          "w_glu", "b_glu", "peer_wq", "peer_subkeys", "peer_u", "peer_v"]


def kernel(**inputs):
    import numpy as _np
    import concourse.bacc as _bacc
    from concourse import mybir as _mybir
    from concourse.bass_utils import run_bass_kernel_spmd as _run

    nc = _bacc.Bacc("TRN2", target_bir_lowering=False, num_devices=1)
    arrays, args = {}, {}
    for name, value in [(n, inputs[n]) for n in INPUTS] + list(constants().items()):
        v = _np.ascontiguousarray(value)
        arrays[f"in_{name}"] = v
        args[name] = nc.dram_tensor(f"in_{name}", v.shape, _mybir.dt.from_np(v.dtype), kind="ExternalInput").ap()
    out = nc.dram_tensor("out_0", (1, S, D), _mybir.dt.float32, kind="ExternalOutput").ap()
    build(nc, args, out)
    r = _run(nc, [arrays], core_ids=[0])
    return r.results[0]["out_0"]
```

```python
import math
from contextlib import ExitStack

import numpy as np

import concourse.bass as bass
from concourse import mybir

ALU = mybir.AluOpType
ACT = mybir.ActivationFunctionType
AX = mybir.AxisListType
F32 = mybir.dt.float32
I32 = mybir.dt.int32
U32 = mybir.dt.uint32

P = 128
D = 1024
KD = D // P
S = 512
T = S // P
DEPTH = 2
HEADS = 6
HD = 64
SWA = HEADS * HD
S5C = 256
GROUPS = 16
STATE = 64
GC = 16
SJ = GROUPS * STATE // P
NOPE = 64
ROPE = 32
QK = NOPE + ROPE
QLORA = 256
KVLORA = 128
COLS = 3 * SWA + S5C + QLORA + KVLORA + ROPE
U0 = 3 * SWA
CQ0 = U0 + S5C
CKV0 = CQ0 + QLORA
KR0 = CKV0 + KVLORA
KEYS = 128
EXPERTS = KEYS * KEYS
PH = 8
TOPK = 16
SLOTS = PH * TOPK
RING = 16
EPS = 1e-6
BUCKETS = 32
MAXDIST = 2048
BRANCHES = ((128, 1), (512, 4), (2048, 16))
NEG = -1e30
LOWEST = -3e38
GELU_C = 2.0 * math.sqrt(2.0 / math.pi)
ROUND = 1.5 * 2.0 ** 23
MOD_W = 256
ROUND13 = 1.5 * 2.0 ** 10
TWO_PI = 6.283185
TOEP = 640


def constants():
    dist = S - 1 - np.arange(TOEP)
    large = 16 + (np.log(np.maximum(dist, 1).astype(np.float32) / np.float32(16))
                  / np.float32(math.log(MAXDIST / 16)) * np.float32(16)).astype(np.int32)
    bucket = np.where(dist < 16, dist, np.minimum(large, BUCKETS - 1))
    mult = sum(((dist >= 0) & (dist % dil == 0) & (dist <= window)).astype(np.float32)
               for window, dil in BRANCHES)
    rows = np.zeros((BUCKETS + 2, TOEP), np.float32)
    for b in range(BUCKETS):
        rows[b] = (bucket == b) & (dist >= 0)
    rows[BUCKETS] = np.where(mult > 0, np.log(np.maximum(mult, 1)), NEG)
    rows[BUCKETS + 1] = np.where(dist >= 0, 0.0, NEG)
    sel = np.zeros((BUCKETS + 2, HEADS + 1), np.float32)
    sel[BUCKETS, :HEADS] = 1.0
    sel[BUCKETS + 1, HEADS] = 1.0
    inv_freq = np.float32(10000.0) ** (-np.arange(0, ROPE, 2, dtype=np.float32) / np.float32(ROPE))
    ang = np.arange(S, dtype=np.float32)[:, None] * inv_freq.astype(np.float32)[None, :]
    states = np.arange(P)
    blk = np.zeros((P, SJ, 8), np.float32)
    for j in range(SJ):
        blk[states, j, (2 * j + states // STATE) % 8] = 1.0
    rowpar = np.zeros((P, P), np.float32)
    for r in range(P):
        half = (r // GC) % 2
        rowpar[r, half * STATE:(half + 1) * STATE] = 1.0
    means = np.zeros((P, 16), np.float32)
    means[:, :12] = 1.0 / HD
    means[:, 12] = 1.0 / QLORA
    means[:, 13] = 1.0 / KVLORA
    means[:, 14] = 1.0 / ROPE
    means[:, 15] = 1.0
    return {
        "c_rows": rows, "c_sel": sel,
        "c_eye": np.eye(P, dtype=np.float32), "c_flip": np.eye(P, dtype=np.float32)[::-1].copy(),
        "c_cos": np.cos(ang).astype(np.float32), "c_sin": np.sin(ang).astype(np.float32),
        "c_blk": blk.reshape(P, SJ * 8), "c_rowpar": rowpar, "c_means": means,
        "c_steps": np.broadcast_to(np.arange(1, S + 1, dtype=np.float32), (P, S)).copy(),
        "c_list": np.broadcast_to(np.arange(TOPK, dtype=np.float32), (P, TOPK)).copy(),
    }


class Link:

    def __init__(self, eng, own):
        self.eng, self.own, self.count = eng, own, {}

    def mark(self, ins, sem=None):
        sem = sem or self.own
        n = self.count[sem.name] = self.count.get(sem.name, 0) + 1
        ins.then_inc(sem, 1)
        return n

    def __call__(self, ins, sem=None):
        n = self.mark(ins, sem)
        self.eng.wait_ge(sem or self.own, n)


class Turn:

    def __init__(self, eng, sem):
        self.eng, self.sem, self.n = eng, sem, 0

    def __call__(self, ins):
        self.n += 1
        ins.then_inc(self.sem, 1)
        self.eng.wait_ge(self.sem, self.n)

    def done(self):
        self.eng.sem_clear(self.sem)


def gelu_terms(link, dve, y, g, cap=80.0):
    link(dve.tensor_tensor(g, y, y, ALU.mult))
    link(dve.tensor_scalar(g, g, 0.044715, 1.0, ALU.mult, ALU.add))
    link(dve.tensor_tensor(g, g, y, ALU.mult))
    link(dve.tensor_scalar(g, g, -GELU_C, cap, ALU.mult, ALU.min))


def s5_block(nc, a, layer, link, sem_of, PS, PRJ, MOD, CB, H, HT, eye, blk, rowpar):
    with ExitStack() as st:
        def sb(name, shape, dt=F32):
            return st.enter_context(nc.sbuf_tensor(name, shape, dt))

        steps = sb("steps", [P, S])
        UT = sb("UT", [P, 2, S])
        BR = sb("BR", [P, SJ, GC])
        BI = sb("BI", [P, SJ, GC])
        BB = sb("BB", [P, 2, SJ, GC])
        BT = sb("BT", [P, SJ, GC])
        BP = sb("BP", [P, 2, SJ, P])
        BW = sb("BW", [P, 2, SJ, P])
        CP = sb("CP", [P, 2, 2, 2, STATE])
        CW = sb("CW", [P, 3, SJ, 32])
        K = sb("K", [P, 20, SJ])
        F = sb("F", [P, 3, S])
        MW = sb("MW", [P, 2, KD, MOD_W])
        FT = sb("FT", [P, 2, S])
        SN = sb("SN", [P, 2, S])
        CS = sb("CS", [P, 2, S])
        Z, QQ = HT[:, 0:4, :], HT[:, 6:8, :]
        PR = sb("PR", [P, 2, 4, S])
        DG = sb("DG", [P, 2, S5C])
        WG = sb("WG", [P, 2, S5C])
        Y = CS[:, :, :].rearrange("p a (b c) -> p (a b) c", c=S5C)
        G = HT[:, 4:6, :].rearrange("p a (b c) -> p (a b) c", c=S5C)
        GT = UT
        ar, ai, ldt, dt, mag, w, tmp, sn, s2, cs, lr, li, den, cr, ci, t2, whi, wlo, acts, mdt = (
            K[:, i, :] for i in range(20))
        (loads, gate_in, ut_tp, ut_ev, k_act, k_dve, pad, bw_tp, bw_ev, cw_ready, phase, tab, tab_used, bu_mm,
         prod, y_mm, y_ready, e_ready, g_ready, gt_tp, gt_ev, glu_mm, glu_pre, glu_e, rotated, f_used) = (
            sem_of(f"s5_{s}") for s in
            ("loads", "gate_in", "ut_tp", "ut_ev", "k_act", "k_dve", "pad", "bw_tp", "bw_ev", "cw_ready", "phase",
             "tab", "tab_used", "bu_mm", "prod", "y_mm", "y_ready", "e_ready", "g_ready", "gt_tp", "gt_ev",
             "glu_mm", "glu_pre", "glu_e", "rotated", "f_used"))
        frac, mod_mm, mod_ev = sem_of("s5_frac"), sem_of("s5_mod_mm"), sem_of("s5_mod_ev")
        mod_in = [sem_of(f"s5_mod_in{i}") for i in range(2)]
        first_col = 2 * D
        mod_chunks = (6 * D - first_col) // MOD_W
        act_step, pool_step = sem_of("s5_act_step"), sem_of("s5_pool_step")
        n_loads = 0
        with nc.Block() as block:
            @block.sync
            def _(sp):
                nonlocal n_loads
                col = dict(allow_slow_non_contiguous=True)

                def load(dst, src, **k):
                    nonlocal n_loads
                    n_loads += 1
                    sp.dma_start(dst, src, **k).then_inc(loads, 16)

                load(ar, a["s5_a_re"][layer].rearrange("(j g) p -> (g p) j", g=2), **col)
                load(ai, a["s5_a_im"][layer].rearrange("(j g) p -> (g p) j", g=2), **col)
                for half in range(2):
                    load(ldt[half * STATE:(half + 1) * STATE, :],
                         a["s5_log_dt"][layer].rearrange("(j g) -> g j", g=2)[half, :].partition_broadcast(STATE),
                         **col)
                load(BR[:, :, :], a["s5_b_re"][layer].rearrange("(j g) p c -> (g p) j c", g=2))
                load(BI[:, :, :], a["s5_b_im"][layer].rearrange("(j g) p c -> (g p) j c", g=2))
                for i, name in enumerate(("s5_c_re", "s5_c_im")):
                    src = a[name][layer].rearrange("(h g) c p -> (g c) h p", h=2)
                    for copy in range(2):
                        load(CP[:, i, :, copy, :], src)
                load(steps[:, :], a["c_steps"])
                sp.dma_start(DG[:, 0, :], a["s5_d"][layer, :].partition_broadcast(P)).then_inc(gate_in, 16)
                sp.dma_start(DG[:, 1, :], a["b_glu"][layer, :].partition_broadcast(P)).then_inc(gate_in, 16)
                sp.dma_start(WG[:, :, :], a["w_glu"][layer].rearrange("(k p) n -> p k n", p=P)).then_inc(gate_in, 16)
                for n in range(mod_chunks):
                    if n >= 2:
                        sp.wait_ge(mod_mm, n - 1)
                    lo = first_col + n * MOD_W
                    sp.dma_start(MW[:, n % 2, :, :],
                                 a["w_ada"][layer, :, lo:lo + MOD_W].rearrange("(k p) n -> p k n", p=P))\
                        .then_inc(mod_in[n % 2], 16)

            @block.gpsimd
            def _(pool):
                slink = Link(pool, pool_step)
                pool.wait_ge(k_dve, 3)
                for j in range(SJ):
                    A, R = F[:, 0, :], F[:, 1, :]
                    ft = FT[:, j % 2, :]
                    slink(pool.tensor_scalar(A, steps[:, :], whi[:, j:j + 1], None, ALU.mult))
                    slink(pool.tensor_scalar(R, A, ROUND, None, ALU.add))
                    slink(pool.tensor_scalar(R, R, ROUND, None, ALU.subtract))
                    if j >= 2:
                        pool.wait_ge(f_used, 2 * (j - 1))
                    slink(pool.tensor_tensor(ft, A, R, ALU.subtract), frac)

            @block.scalar
            def _(act):
                slink = Link(act, act_step)
                act.wait_ge(loads, 16 * n_loads)
                slink(act.activation(dt, ldt, ACT.Exp))
                act.activation(mdt, dt, ACT.Copy).then_inc(k_act, 1)
                act.wait_ge(k_dve, 1)
                act.activation(mag, tmp, ACT.Exp).then_inc(k_act, 1)
                act.wait_ge(k_dve, 2)
                act.activation(sn, w, ACT.Sin, scale=TWO_PI).then_inc(k_act, 1)
                act.activation(s2, w, ACT.Sin, scale=TWO_PI / 2).then_inc(k_act, 1)
                for i in range(2):
                    act.wait_ge(ut_tp, i + 1)
                    act.activation(UT[:, i, :], PS[:, 6 + i, :], ACT.Copy).then_inc(ut_ev, 1)
                for i in range(16):
                    act.wait_ge(bw_tp, i + 1)
                    act.activation(BW[:, i // SJ, i % SJ, :], PS[:, 4 + i % 4, 0:P], ACT.Copy).then_inc(bw_ev, 1)
                for i in range(4):
                    act.wait_ge(bw_tp, 17 + i)
                    part, h = i // 2, i % 2
                    src = PS[:, 4 + i % 4, 0:P].rearrange("p (j c) -> p j c", c=32)
                    if part == 0:
                        act.activation(CW[:, 0, 4 * h:4 * h + 4, :], src, ACT.Copy).then_inc(cw_ready, 1)
                        act.activation(CW[:, 1, 4 * h:4 * h + 4, :], src, ACT.Copy, scale=-1.0).then_inc(cw_ready, 1)
                    else:
                        act.activation(CW[:, 2, 4 * h:4 * h + 4, :], src, ACT.Copy, scale=-1.0).then_inc(cw_ready, 1)
                for j in range(SJ):
                    b = j % 2
                    act.wait_ge(phase, j + 1)
                    if j >= 2:
                        act.wait_ge(tab_used, j - 1)
                    act.activation(SN[:, b, :], FT[:, b, :], ACT.Sin, scale=TWO_PI).then_inc(f_used, 1)
                    act.activation(QQ[:, 0, :], FT[:, b, :], ACT.Sin, scale=TWO_PI / 2).then_inc(f_used, 1)
                    act.wait_ge(f_used, 2 * j + 2)
                    slink(act.activation(QQ[:, 1, :], QQ[:, 0, :], ACT.Square, scale=math.sqrt(2.0)))
                    act.activation(CS[:, b, :], QQ[:, 1, :], ACT.Copy, scale=-1.0, bias=1.0).then_inc(tab, 1)
                    act.wait_ge(tab, j + 1)
                act.wait_ge(y_ready, 1)
                act.activation(G[:, :, :], G[:, :, :], ACT.Exp).then_inc(e_ready, 1)
                for i in range(2):
                    act.wait_ge(gt_tp, i + 1)
                    act.activation(GT[:, i, :], PS[:, 6 + i, :], ACT.Copy).then_inc(gt_ev, 1)
                act.wait_ge(glu_pre, 1)
                act.activation(G[:, :, :], G[:, :, :], ACT.Exp, scale=-1.0).then_inc(glu_e, 1)

            @block.tensor
            def _(pe):
                for i in range(2):
                    for t in range(T):
                        last = pe.transpose(PS[:, 6 + i, t * P:(t + 1) * P], PRJ[:, t, U0 + i * P:U0 + (i + 1) * P],
                                            eye[:, :])
                    last.then_inc(ut_tp, 1)
                pe.wait_ge(ut_ev, 2)
                pe.wait_ge(pad, 2)
                for i in range(16):
                    if i >= 4:
                        pe.wait_ge(bw_ev, i - 3)
                    pe.transpose(PS[:, 4 + i % 4, 0:P], BP[:, i // SJ, i % SJ, :], eye[:, :]).then_inc(bw_tp, 1)
                pe.wait_ge(pad, 3)
                for i in range(4):
                    pe.wait_ge(bw_ev, 13 + i)
                    pe.transpose(PS[:, 4 + i % 4, 0:P], CP[:, i // 2, i % 2, :, :].rearrange("p a b -> p (a b)"),
                                 eye[:, :]).then_inc(bw_tp, 1)
                pe.wait_ge(ut_ev, 2)

                def drive(j):
                    if j >= 2:
                        pe.wait_ge(rotated, j - 1)
                    for c in range(2):
                        last = pe.matmul(PS[:, 2 * (j % 2) + c, :], BW[:, c, j, :], UT[:, j // 4, :],
                                         start=True, stop=True)
                    last.then_inc(bu_mm, 1)

                def modulate(n):
                    pe.wait_ge(mod_in[n % 2], 16 * (n // 2 + 1))
                    if n >= 2:
                        pe.wait_ge(mod_ev, n - 1)
                    for k in range(KD):
                        last = pe.matmul(PS[:, 6 + n % 2, 0:MOD_W], CB[:, k, :], MW[:, n % 2, k, :],
                                         start=(k == 0), stop=(k == KD - 1))
                    last.then_inc(mod_mm, 1)

                drive(0)
                pe.wait_ge(cw_ready, 6)
                for j in range(SJ):
                    if j + 1 < SJ:
                        drive(j + 1)
                    modulate(2 * j)
                    modulate(2 * j + 1)
                    pe.wait_ge(prod, j + 1)
                    for t in range(T):
                        for q, wt in enumerate((0, 1, 2, 2)):
                            y0 = (t % 2) * S5C + 32 * j
                            last = pe.matmul(PS[:, 4 + t // 2, y0:y0 + 32], PR[:, j % 2, q, t * P:(t + 1) * P],
                                             CW[:, wt, j, :], start=(q == 0), stop=(q == 3))
                    last.then_inc(y_mm, 1)
                pe.wait_ge(g_ready, 1)
                pe.wait_ge(mod_ev, mod_chunks)
                for i in range(2):
                    for t in range(T):
                        last = pe.transpose(PS[:, 6 + i, t * P:(t + 1) * P], Y[:, t, i * P:(i + 1) * P], eye[:, :])
                    last.then_inc(gt_tp, 1)
                pe.wait_ge(gate_in, 48)
                pe.wait_ge(gt_ev, 2)
                for t in range(T):
                    for k in range(2):
                        last = pe.matmul(PS[:, t // 2, (t % 2) * S5C:(t % 2 + 1) * S5C], GT[:, k, t * P:(t + 1) * P],
                                         WG[:, k, :], start=(k == 0), stop=(k == 1))
                last.then_inc(glu_mm, 1)

            @block.vector
            def _(dve):
                link.eng = dve
                dve.wait_ge(k_act, 1)
                link(dve.tensor_tensor(tmp, ar, mdt, ALU.mult), k_dve)
                link(dve.tensor_tensor(w, ai, mdt, ALU.mult))
                link(dve.tensor_scalar(w, w, 1.0 / (2.0 * math.pi), None, ALU.mult))
                link(dve.tensor_scalar(t2, w, ROUND, None, ALU.add))
                link(dve.tensor_scalar(t2, t2, ROUND, None, ALU.subtract))
                link(dve.tensor_tensor(w, w, t2, ALU.subtract), k_dve)
                link(dve.tensor_scalar(whi, w, ROUND13, None, ALU.add))
                link(dve.tensor_scalar(whi, whi, ROUND13, None, ALU.subtract))
                link(dve.tensor_tensor(wlo, w, whi, ALU.subtract), k_dve)
                dve.wait_ge(k_act, 4)
                link(dve.tensor_tensor(cs, s2, s2, ALU.mult))
                link(dve.tensor_scalar(cs, cs, -2.0, 1.0, ALU.mult, ALU.add))
                link(dve.tensor_tensor(lr, mag, cs, ALU.mult))
                link(dve.tensor_scalar(lr, lr, -1.0, None, ALU.add))
                link(dve.tensor_tensor(li, mag, sn, ALU.mult))
                link(dve.tensor_tensor(den, ar, ar, ALU.mult))
                link(dve.tensor_tensor(t2, ai, ai, ALU.mult))
                link(dve.tensor_tensor(den, den, t2, ALU.add))
                link(dve.reciprocal(den, den))
                link(dve.tensor_tensor(cr, lr, ar, ALU.mult))
                link(dve.tensor_tensor(t2, li, ai, ALU.mult))
                link(dve.tensor_tensor(cr, cr, t2, ALU.add))
                link(dve.tensor_tensor(cr, cr, den, ALU.mult))
                link(dve.tensor_tensor(ci, li, ar, ALU.mult))
                link(dve.tensor_tensor(t2, lr, ai, ALU.mult))
                link(dve.tensor_tensor(ci, ci, t2, ALU.subtract))
                link(dve.tensor_tensor(ci, ci, den, ALU.mult))
                crb = cr.unsqueeze(2).to_broadcast([P, SJ, GC])
                cib = ci.unsqueeze(2).to_broadcast([P, SJ, GC])
                link(dve.tensor_tensor(BB[:, 0, :, :], BR[:, :, :], crb, ALU.mult))
                link(dve.tensor_tensor(BT[:, :, :], BI[:, :, :], cib, ALU.mult))
                link(dve.tensor_tensor(BB[:, 0, :, :], BB[:, 0, :, :], BT[:, :, :], ALU.subtract))
                link(dve.tensor_tensor(BB[:, 1, :, :], BI[:, :, :], crb, ALU.mult))
                link(dve.tensor_tensor(BT[:, :, :], BR[:, :, :], cib, ALU.mult))
                link(dve.tensor_tensor(BB[:, 1, :, :], BB[:, 1, :, :], BT[:, :, :], ALU.add))
                for i in range(2):
                    link(dve.tensor_tensor(BP[:, i, :, :].rearrange("p j (b c) -> p j b c", c=GC),
                                           BB[:, i, :, :].unsqueeze(2).to_broadcast([P, SJ, 8, GC]),
                                           blk[:, :, :].unsqueeze(3).to_broadcast([P, SJ, 8, GC]), ALU.mult), pad)
                cp = CP[:, :, :, :, :].rearrange("p i h a b -> p (i h) (a b)")
                link(dve.tensor_tensor(cp, cp, rowpar[:, :].unsqueeze(1).to_broadcast([P, 4, P]), ALU.mult), pad)
                def table(j):
                    ft, r = FT[:, j % 2, :], F[:, 2, :]
                    dve.wait_ge(frac, j + 1)
                    link(dve.scalar_tensor_tensor(ft, steps[:, :], wlo[:, j:j + 1], ft, ALU.mult, ALU.add))
                    link(dve.tensor_scalar(r, ft, ROUND, ROUND, ALU.add, ALU.subtract))
                    link(dve.tensor_tensor(ft, ft, r, ALU.subtract), phase)

                def modulated(n):
                    lo = first_col + n * MOD_W
                    m = MOD[:, lo // D, lo % D:lo % D + MOD_W]
                    dve.wait_ge(mod_mm, n + 1)
                    link(dve.tensor_tensor(m, PS[:, 6 + n % 2, 0:MOD_W], m, ALU.add), mod_ev)

                table(0)
                for j in range(SJ):
                    if j + 1 < SJ:
                        table(j + 1)
                    b = j % 2
                    br, bi = PS[:, 2 * b, :], PS[:, 2 * b + 1, :]
                    c, s = CS[:, b, :], SN[:, b, :]
                    z = [Z[:, i, :] for i in range(4)]
                    dve.wait_ge(tab, j + 1)
                    dve.wait_ge(bu_mm, j + 1)
                    link(dve.tensor_tensor(z[0], br, c, ALU.mult))
                    link(dve.tensor_tensor(z[1], bi, s, ALU.mult))
                    link(dve.tensor_tensor(z[0], z[0], z[1], ALU.add))
                    link(dve.tensor_tensor(z[1], bi, c, ALU.mult))
                    link(dve.tensor_tensor(z[2], br, s, ALU.mult), rotated)
                    link(dve.tensor_tensor(z[1], z[1], z[2], ALU.subtract))
                    m = mag[:, j:j + 1].to_broadcast([P, S])
                    link(dve.tensor_tensor_scan(z[2], m, z[0], 0.0, ALU.mult, ALU.add))
                    link(dve.tensor_tensor_scan(z[3], m, z[1], 0.0, ALU.mult, ALU.add))
                    if j >= 2:
                        dve.wait_ge(y_mm, j - 1)
                    link(dve.tensor_tensor(PR[:, b, 0, :], z[2], c, ALU.mult))
                    link(dve.tensor_tensor(PR[:, b, 1, :], z[3], s, ALU.mult))
                    link(dve.tensor_tensor(PR[:, b, 2, :], z[3], c, ALU.mult))
                    link(dve.tensor_tensor(PR[:, b, 3, :], z[2], s, ALU.mult), prod)
                    dve.sem_inc(tab_used, 1)
                    modulated(2 * j)
                    modulated(2 * j + 1)
                dve.wait_ge(gate_in, 48)
                dve.wait_ge(y_mm, SJ)
                u = PRJ[:, :, U0:U0 + S5C]
                link(dve.tensor_tensor(Y[:, :, :], u, DG[:, 0, :].unsqueeze(1).to_broadcast([P, T, S5C]), ALU.mult))
                link(dve.tensor_tensor(Y[:, :, :], Y[:, :, :],
                                       PS[:, 4:6, :].rearrange("p b (t c) -> p (b t) c", c=S5C), ALU.add))
                gelu_terms(link, dve, Y[:, :, :], G[:, :, :])
                dve.sem_inc(y_ready, 1)
                dve.wait_ge(e_ready, 1)
                link(dve.tensor_scalar(G[:, :, :], G[:, :, :], 1.0, None, ALU.add))
                link(dve.reciprocal(G[:, :, :], G[:, :, :]))
                link(dve.tensor_tensor(Y[:, :, :], Y[:, :, :], G[:, :, :], ALU.mult), g_ready)
                dve.wait_ge(glu_mm, 1)
                link(dve.tensor_tensor(G[:, :, :], PS[:, 0:2, :].rearrange("p b (t c) -> p (b t) c", c=S5C),
                                       DG[:, 1, :].unsqueeze(1).to_broadcast([P, T, S5C]), ALU.add))
                link(dve.tensor_scalar(G[:, :, :], G[:, :, :], -80.0, None, ALU.max), glu_pre)
                dve.wait_ge(glu_e, 1)
                link(dve.tensor_scalar(G[:, :, :], G[:, :, :], 1.0, None, ALU.add))
                link(dve.reciprocal(G[:, :, :], G[:, :, :]))
                link(dve.tensor_tensor(H[:, :, SWA:SWA + S5C], Y[:, :, :], G[:, :, :], ALU.mult))


def attention(nc, a, layer, link, sem_of, PS, PRJ, H, HT, eye, means, BM, cosT, sinT, RS, V0, rsqrt):
    with ExitStack() as st:
        def sb(name, shape, dt=F32):
            return st.enter_context(nc.sbuf_tensor(name, shape, dt))

        QM = sb("QM", [P, T, HEADS, QK])
        KC = sb("KC", [P, T, HEADS, QK])
        KV = sb("KV", [P, T, HEADS, NOPE + HD])
        GQK = sb("GQK", [P, 2, HD])
        GM = sb("GM", [P, 2, QK])
        GC_ = sb("GC_", [P, QLORA + KVLORA])
        SQ = HT[:, :, :].rearrange("p k s -> p (k s)")
        gains, w_in, sq, sq2, cn, tp, ev, mm, mev, sq3, sq4 = (sem_of(f"at_{s}") for s in (
            "gains", "w", "sq", "sq2", "cn", "tp", "ev", "mm", "mev", "sq3", "sq4"))
        with ExitStack() as lat:
            WUQ = lat.enter_context(nc.sbuf_tensor("WUQ", [P, 2, HEADS * QK], F32))
            WUKV = lat.enter_context(nc.sbuf_tensor("WUKV", [P, HEADS * (NOPE + HD)], F32))
            CT = lat.enter_context(nc.sbuf_tensor("CT", [P, 3, S], F32))
            with nc.Block() as block:
                @block.sync
                def _(sp):
                    for dst, name in ((GQK[:, 0, :], "swa_q_gain"), (GQK[:, 1, :], "swa_k_gain"),
                                      (GM[:, 0, :], "mla_q_gain"), (GM[:, 1, :], "mla_k_gain"),
                                      (GC_[:, 0:QLORA], "mla_q_lora_gain"), (GC_[:, QLORA:], "mla_kv_lora_gain")):
                        sp.dma_start(dst, a[name][layer, :].partition_broadcast(P)).then_inc(gains, 16)
                    sp.dma_start(WUQ[:, :, :], a["w_uq"][layer].rearrange("(k p) n -> p k n", p=P)).then_inc(w_in, 16)
                    sp.dma_start(WUKV[:, :], a["w_ukv"][layer]).then_inc(w_in, 16)

                @block.scalar
                def _(act):
                    sq_step = sem_of("at_sq_step")
                    for t in range(T):
                        act.activation(SQ[:, t * 768:(t + 1) * 768], PRJ[:, t, 0:768], ACT.Square).then_inc(sq, 1)
                    for t in range(T):
                        for i, (lo, hi) in enumerate(((CQ0, CKV0), (CKV0, KR0), (KR0, COLS))):
                            c = t * 15 + 12 + i
                            if t or i:
                                act.wait_ge(sq2, 3 * t + i)
                            act.activation(SQ[:, 3072:3072 + hi - lo], PRJ[:, t, lo:hi], ACT.Square,
                                           accum_out=V0[:, c:c + 1]).then_inc(sq2, 1)
                    for i in range(3):
                        act.wait_ge(tp, i + 1)
                        act.activation(CT[:, i, :], PS[:, i, :], ACT.Copy).then_inc(ev, 1)
                    for t in range(T):
                        for n in range(4):
                            i = 4 * t + n
                            act.wait_ge(mm, i + 1)
                            if n < 2:
                                act.activation(QM[:, t, 3 * n:3 * n + 3, :], PS[:, 4 + n, 0:3 * QK].rearrange(
                                    "p (h c) -> p h c", c=QK), ACT.Copy).then_inc(mev, 1)
                            else:
                                m = n - 2
                                act.activation(KV[:, t, 3 * m:3 * m + 3, :], PS[:, 4 + n, 0:384].rearrange(
                                    "p (h c) -> p h c", c=P), ACT.Copy).then_inc(mev, 1)

                @block.vector
                def _(dve):
                    link.eng = dve
                    v15 = V0[:, 0:60].rearrange("p (t c) -> p t c", c=15)
                    for t in range(T):
                        dve.wait_ge(sq, t + 1)
                        link(dve.tensor_reduce(v15[:, t, 0:12],
                                               SQ[:, t * 768:(t + 1) * 768].rearrange("p (h c) -> p h c", c=HD),
                                               AX.X, ALU.add))
                    dve.wait_ge(sq2, 12)
                    link(dve.tensor_tensor(v15, v15, means[:, 0:15].unsqueeze(1).to_broadcast([P, T, 15]), ALU.mult))
                    link(dve.tensor_scalar(V0[:, 0:60], V0[:, 0:60], EPS, None, ALU.add))
                    rsqrt(link, 60)
                    r15 = RS[:, 0:60].rearrange("p (t c) -> p t c", c=15)
                    dve.wait_ge(gains, 96)
                    for t in range(T):
                        for lo, hi, c, g in ((CQ0, CKV0, 12, 0), (CKV0, KR0, 13, QLORA)):
                            link(dve.scalar_tensor_tensor(PRJ[:, t, lo:hi], PRJ[:, t, lo:hi],
                                                          RS[:, 15 * t + c:15 * t + c + 1], GC_[:, g:g + hi - lo],
                                                          ALU.mult, ALU.mult), cn)
                        link(dve.scalar_tensor_tensor(PRJ[:, t, KR0:COLS], PRJ[:, t, KR0:COLS],
                                                      RS[:, 15 * t + 14:15 * t + 15], GM[:, 1, NOPE:QK],
                                                      ALU.mult, ALU.mult))
                    link(dve.tensor_scalar(GQK[:, 0, :], GQK[:, 0, :], HD ** -0.5, None, ALU.mult))
                    link(dve.tensor_scalar(GM[:, 0, :], GM[:, 0, :], QK ** -0.5, None, ALU.mult))
                    for i in range(2):
                        x = PRJ[:, :, i * SWA:(i + 1) * SWA].rearrange("p t (h c) -> p t h c", c=HD)
                        r = r15[:, :, 6 * i:6 * i + 6].unsqueeze(3).to_broadcast([P, T, HEADS, HD])
                        g = GQK[:, i, :].unsqueeze(1).unsqueeze(1).to_broadcast([P, T, HEADS, HD])
                        link(dve.tensor_tensor(x, x, r, ALU.mult))
                        link(dve.tensor_tensor(x, x, g, ALU.mult))

                @block.tensor
                def _(pe):
                    pe.wait_ge(cn, 8)
                    for i in range(3):
                        for t in range(T):
                            last = pe.transpose(PS[:, i, t * P:(t + 1) * P],
                                                PRJ[:, t, CQ0 + i * P:CQ0 + (i + 1) * P], eye[:, :])
                        last.then_inc(tp, 1)
                    pe.wait_ge(w_in, 32)
                    pe.wait_ge(ev, 3)
                    for t in range(T):
                        rows = slice(t * P, (t + 1) * P)
                        if t:
                            pe.wait_ge(mev, 4 * t)
                        for n in range(2):
                            for k in range(2):
                                last = pe.matmul(PS[:, 4 + n, 0:288], CT[:, k, rows], WUQ[:, k, n * 288:(n + 1) * 288],
                                                 start=(k == 0), stop=(k == 1))
                            last.then_inc(mm, 1)
                        for n in range(2):
                            pe.matmul(PS[:, 6 + n, 0:384], CT[:, 2, rows], WUKV[:, n * 384:(n + 1) * 384],
                                      start=True, stop=True).then_inc(mm, 1)

        with nc.Block() as block:
            @block.scalar
            def _(act):
                act.activation(SQ[:, 0:T * HEADS * QK], QM[:, :, :, :].rearrange("p t h c -> p (t h c)"),
                               ACT.Square).then_inc(sq3, 1)
                act.activation(SQ[:, 2304:2304 + T * HEADS * NOPE].rearrange("p (t h c) -> p (t h) c", h=HEADS, c=NOPE),
                               KV[:, :, :, 0:NOPE].rearrange("p t h c -> p (t h) c"), ACT.Square).then_inc(sq4, 1)

            @block.vector
            def _(dve):
                link.eng = dve
                n = T * HEADS
                q2 = SQ[:, 0:n * QK].rearrange("p (m c) -> p m c", c=QK)
                k2 = SQ[:, 2304:2304 + n * NOPE].rearrange("p (m c) -> p m c", c=NOPE)
                dve.wait_ge(sq3, 1)
                link(dve.tensor_reduce(V0[:, 0:n], q2[:, :, 0:NOPE], AX.X, ALU.add))
                link(dve.tensor_reduce(V0[:, n:2 * n], q2[:, :, NOPE:QK], AX.X, ALU.add))
                dve.wait_ge(sq4, 1)
                link(dve.tensor_reduce(V0[:, 2 * n:3 * n], k2, AX.X, ALU.add))
                for i, m in enumerate((NOPE, ROPE, NOPE)):
                    link(dve.tensor_scalar(V0[:, i * n:(i + 1) * n], V0[:, i * n:(i + 1) * n], 1.0 / m, EPS,
                                           ALU.mult, ALU.add))
                rsqrt(link, 3 * n)
                qm = QM[:, :, :, :].rearrange("p t h c -> p (t h) c")
                kc = KC[:, :, :, :].rearrange("p t h c -> p (t h) c")
                kv = KV[:, :, :, 0:NOPE].rearrange("p t h c -> p (t h) c")
                for x, y, w, r, g in ((qm[:, :, 0:NOPE], qm[:, :, 0:NOPE], NOPE, 0, GM[:, 0, 0:NOPE]),
                                      (qm[:, :, NOPE:QK], qm[:, :, NOPE:QK], ROPE, 1, GM[:, 0, NOPE:QK]),
                                      (kv, kc[:, :, 0:NOPE], NOPE, 2, GM[:, 1, 0:NOPE])):
                    rb = RS[:, r * n:(r + 1) * n].unsqueeze(2).to_broadcast([P, n, w])
                    link(dve.tensor_tensor(y, x, rb, ALU.mult))
                    link(dve.tensor_tensor(y, y, g.unsqueeze(1).to_broadcast([P, n, w]), ALU.mult))
                half = ROPE // 2
                for x, y, h in ((QM[:, :, :, NOPE:QK], QM[:, :, :, NOPE:QK], HEADS),
                                (PRJ[:, :, KR0:COLS].unsqueeze(2), None, 1)):
                    m = T * h * half
                    tmp = [SQ[:, i * m:(i + 1) * m].rearrange("p (t h c) -> p t h c", t=T, h=h) for i in range(4)]
                    cb = cosT[:, :, :].unsqueeze(2).to_broadcast([P, T, h, half])
                    sb_ = sinT[:, :, :].unsqueeze(2).to_broadcast([P, T, h, half])
                    x1, x2 = x[:, :, :, 0:half], x[:, :, :, half:ROPE]
                    link(dve.tensor_tensor(tmp[0], x1, cb, ALU.mult))
                    link(dve.tensor_tensor(tmp[1], x2, sb_, ALU.mult))
                    link(dve.tensor_tensor(tmp[2], x1, sb_, ALU.mult))
                    link(dve.tensor_tensor(tmp[3], x2, cb, ALU.mult))
                    if y is None:
                        y = PRJ[:, :, KR0:COLS].unsqueeze(2)
                    link(dve.tensor_tensor(y[:, :, :, 0:half], tmp[0], tmp[1], ALU.subtract))
                    link(dve.tensor_tensor(y[:, :, :, half:ROPE], tmp[2], tmp[3], ALU.add))
                link(dve.tensor_copy(KC[:, :, :, NOPE:QK],
                                     PRJ[:, :, KR0:COLS].unsqueeze(2).to_broadcast([P, T, HEADS, ROPE])))

        QT = sb("QT", [QK, 2 * HEADS, S])
        KT = sb("KT", [QK, 2 * HEADS, S])
        htp, hev_a, hev_d = sem_of("at_htp"), sem_of("at_hev_a"), sem_of("at_hev_d")
        lg, lmax, pexp, ptp, pev, omm, odone = (sem_of(f"at_{s}") for s in (
            "logits", "max", "exp", "ptp", "pev", "omm", "odone"))

        def head_source(i):
            h, isk = i // 2, i % 2
            dst = (KT if isk else QT)
            if h < HEADS:
                return dst[0:HD, h, :], lambda t: PRJ[:, t, isk * SWA + h * HD:isk * SWA + (h + 1) * HD], HD
            return dst[:, h, :], lambda t: (KC if isk else QM)[:, t, h - HEADS, :], QK

        pairs = [(h, t) for h in range(2 * HEADS) for t in range(T)]
        with nc.Block() as block:
            @block.tensor
            def _(pe):
                for i in range(4 * HEADS):
                    dst, src, w = head_source(i)
                    if i >= 4:
                        pe.wait_ge((hev_a, hev_d)[i % 2], (i - 4) // 2 + 1)
                    for t in range(T):
                        last = pe.transpose(PS[0:w, i % 4, t * P:(t + 1) * P], src(t), eye[:, :])
                    last.then_inc(htp, 1)
                pe.wait_ge(hev_a, 2 * HEADS)
                pe.wait_ge(hev_d, 2 * HEADS)

                def logits(i):
                    h, t = pairs[i]
                    w = HD if h < HEADS else QK
                    n = (t + 1) * P
                    if i >= 2:
                        pe.wait_ge(lmax, i - 1)
                    pe.matmul(PS[:, i % 2, 0:n], QT[0:w, h, t * P:(t + 1) * P], KT[0:w, h, 0:n],
                              start=True, stop=True).then_inc(lg, 1)

                def weigh(i):
                    h, t = pairs[i]
                    pe.wait_ge(pexp, i + 1)
                    if i >= 2:
                        pe.wait_ge(pev, i - 1)
                    for k in range(t + 1):
                        last = pe.transpose(PS[:, 2 + i % 2, k * P:(k + 1) * P],
                                            HT[:, i % 2, k * P:(k + 1) * P], eye[:, :])
                    last.then_inc(ptp, 1)

                def mix(i):
                    h, t = pairs[i]
                    pe.wait_ge(pev, i + 1)
                    if i >= 2:
                        pe.wait_ge(odone, i - 1)
                    for k in range(t + 1):
                        v = (PRJ[:, k, 2 * SWA + h * HD:2 * SWA + (h + 1) * HD] if h < HEADS
                             else KV[:, k, h - HEADS, NOPE:NOPE + HD])
                        last = pe.matmul(PS[:, 4 + i % 2, 0:HD], HT[:, 2 + i % 2, k * P:(k + 1) * P], v,
                                         start=(k == 0), stop=(k == t))
                    last.then_inc(omm, 1)

                N = len(pairs)
                for i in range(N + 2):
                    if i < N:
                        logits(i)
                    if 1 <= i <= N:
                        weigh(i - 1)
                    if i >= 2:
                        mix(i - 2)

            @block.scalar
            def _(act):
                for i in range(0, 4 * HEADS, 2):
                    dst, _, w = head_source(i)
                    act.wait_ge(htp, i + 1)
                    act.activation(dst, PS[0:w, i % 4, :], ACT.Copy).then_inc(hev_a, 1)

                def evac(i):
                    n = (pairs[i][1] + 1) * P
                    act.wait_ge(ptp, i + 1)
                    if i >= 2:
                        act.wait_ge(omm, i - 1)
                    act.activation(HT[:, 2 + i % 2, 0:n], PS[:, 2 + i % 2, 0:n], ACT.Copy).then_inc(pev, 1)

                for i, (h, t) in enumerate(pairs):
                    n = (t + 1) * P
                    act.wait_ge(lmax, i + 1)
                    act.activation(HT[:, i % 2, 0:n], HT[:, i % 2, 0:n], ACT.Exp, bias=V0[:, 2 * (i % 2):2 * (i % 2) + 1],
                                   accum_out=RS[:, i % 4:i % 4 + 1]).then_inc(pexp, 1)
                    if i >= 1:
                        evac(i - 1)
                evac(len(pairs) - 1)

            @block.vector
            def _(dve):
                link.eng = dve
                for i in range(1, 4 * HEADS, 2):
                    dst, _, w = head_source(i)
                    dve.wait_ge(htp, i + 1)
                    link(dve.tensor_copy(dst, PS[0:w, i % 4, :]), hev_d)

                def finish(i):
                    h, t = pairs[i]
                    c = 8 + i % 2
                    dve.wait_ge(pexp, i + 1)
                    link(dve.reciprocal(V0[:, c:c + 1], RS[:, i % 4:i % 4 + 1]))
                    dve.wait_ge(omm, i + 1)
                    y0 = h * HD if h < HEADS else SWA + S5C + (h - HEADS) * HD
                    link(dve.tensor_scalar(H[:, t, y0:y0 + HD], PS[:, 4 + i % 2, 0:HD], V0[:, c:c + 1], None,
                                           ALU.mult), odone)

                for i, (h, t) in enumerate(pairs):
                    n = (t + 1) * P
                    b = min(h, HEADS)
                    c = 2 * (i % 2)
                    dve.wait_ge(lg, i + 1)
                    if i >= 2:
                        dve.wait_ge(ptp, i - 1)
                    link(dve.tensor_tensor_reduce(HT[:, i % 2, 0:n], PS[:, i % 2, 0:n], BM[:, b, S - n:S], 1.0, LOWEST,
                                                  ALU.add, ALU.max, V0[:, c + 1:c + 2]))
                    link(dve.tensor_scalar(V0[:, c:c + 1], V0[:, c + 1:c + 2], -1.0, None, ALU.mult), lmax)
                    if i >= 2:
                        finish(i - 2)
                finish(len(pairs) - 2)
                finish(len(pairs) - 1)


def peer(nc, a, layer, link, sem_of, PS, X, MOD, H, HT, eye, lst, loff, peer_sems):
    with ExitStack() as st:
        def sb(name, shape, dt=F32):
            return st.enter_context(nc.sbuf_tensor(name, shape, dt))

        IDX = sb("IDX", [P, T, SLOTS], U32)
        GATE = sb("GATE", [P, T, SLOTS])
        SC = sb("SC", [P, T, 2 * PH, P])
        T1 = sb("T1", [P, 2 * PH, TOPK])
        I1f = sb("I1f", [P, 2 * PH, TOPK])
        B1 = sb("B1", [P, PH, TOPK])
        BC = sb("BC", [P, PH, TOPK], U32)
        SU = sb("SU", [P, PH])
        pick = sb("pick", [P, P])
        pick_top = sb("pick_top", [P, TOPK])
        pick_at = sb("pick_at", [P, TOPK], U32)
        g_in, g_exp, idx_done = sem_of("r_g_in"), sem_of("r_g_exp"), sem_of("r_idx_done")
        (ring_in, ring_free, ring_taken, staged, act_ready, gated, out_step, peer_step, peer_exp, top_step,
         diag_ready, pe_sum, zeroed) = peer_sems

        def scratch(wide, small):
            b2, b2f, ex = (small[:, 256 * (i + 1):256 * (i + 2)].rearrange("p (i s) -> p i s", i=2) for i in range(3))
            return (wide.rearrange("p (a k) -> p a k", k=TOPK), small[:, 0:TOPK * TOPK], b2.bitcast(U32), b2f, ex)

        first = scratch(SC[:, 3, :, :].rearrange("p a b -> p (a b)"), SC[:, 2, 0:8, :].rearrange("p a b -> p (a b)"))
        later = scratch(HT[:, 0:4, :].rearrange("p a b -> p (a b)"), HT[:, 4:6, :].rearrange("p a b -> p (a b)"))

        def router(dve, scratch):
            EQ, CA, B2, B2f, EX = scratch

            def top16(slink, values, tops, places):
                slink(dve.max(tops[:, 0:8], values))
                slink(dve.max_index(places[:, 0:8], tops[:, 0:8], values))
                slink(dve.match_replace(values, tops[:, 0:8], values, LOWEST))
                slink(dve.max(tops[:, 8:16], values))
                slink(dve.max_index(places[:, 8:16], tops[:, 8:16], values))

            def best_of_list(t, j):
                slink = Turn(dve, top_step)
                slink(dve.tensor_copy(pick[:, :], SC[:, t, bass.ds(j, 1), :].rearrange("p a k -> p (a k)")))
                top16(slink, pick[:, :], pick_top[:, :], pick_at[:, :])
                slink(dve.tensor_copy(T1[:, bass.ds(j, 1), :].rearrange("p a k -> p (a k)"), pick_top[:, :]))
                slink(dve.tensor_copy(I1f[:, bass.ds(j, 1), :].rearrange("p a k -> p (a k)"), pick_at[:, :]))
                slink.done()

            def best_of_pairs(h):
                slink = Turn(dve, top_step)
                t1 = T1[:, bass.ds(h * 2, 2), :]
                slink(dve.tensor_tensor(CA.rearrange("p (x y) -> p x y", x=TOPK),
                                        t1[:, 0:1, :].rearrange("p a k -> p k a").to_broadcast([P, TOPK, TOPK]),
                                        t1[:, 1:2, :].to_broadcast([P, TOPK, TOPK]), ALU.add))
                top16(slink, CA, pick_top[:, :], pick_at[:, :])
                slink(dve.tensor_copy(B1[:, bass.ds(h, 1), :].rearrange("p a k -> p (a k)"), pick_top[:, :]))
                slink(dve.tensor_copy(BC[:, bass.ds(h, 1), :].rearrange("p a k -> p (a k)"), pick_at[:, :]))
                slink.done()

            def gates_in(t):
                gate = GATE[:, t, :].rearrange("p (h s) -> p h s", h=PH)
                link(dve.tensor_tensor(gate, B1[:, :, :], B1[:, :, 0:1].to_broadcast([P, PH, TOPK]),
                                       ALU.subtract), g_in)

            def experts_of(t):
                gate = GATE[:, t, :].rearrange("p (h s) -> p h s", h=PH)
                bc = BC[:, :, :].rearrange("p h s -> p (h s)")
                link(dve.tensor_scalar(B2[:, 0, :], bc, 4, None, ALU.logical_shift_right))
                link(dve.tensor_scalar(B2[:, 1, :], bc, 15, None, ALU.bitwise_and))
                link(dve.tensor_copy(B2f[:, :, :], B2[:, :, :]))
                i4 = I1f[:, :, :].rearrange("p (h j) k -> p h j k", j=2)
                eq4 = EQ.rearrange("p (h s) k -> p h s k", h=PH)
                for i in range(2):
                    link(dve.tensor_tensor(EQ, B2f[:, i, :].unsqueeze(2).to_broadcast([P, SLOTS, TOPK]),
                                           lst[:, :].unsqueeze(1).to_broadcast([P, SLOTS, TOPK]), ALU.is_equal))
                    link(dve.tensor_tensor(eq4, eq4, i4[:, :, i, :].unsqueeze(2)
                                           .to_broadcast([P, PH, TOPK, TOPK]), ALU.mult))
                    link(dve.tensor_reduce(EX[:, i, :], EQ, AX.X, ALU.add))
                link(dve.scalar_tensor_tensor(EX[:, 0, :], EX[:, 0, :], float(KEYS), EX[:, 1, :],
                                              ALU.mult, ALU.add))
                dve.wait_ge(g_exp, t + 1)
                link(dve.tensor_reduce(SU[:, :], gate, AX.X, ALU.add))
                link(dve.reciprocal(SU[:, :], SU[:, :]))
                link(dve.tensor_tensor(gate, gate, SU[:, :].unsqueeze(2).to_broadcast([P, PH, TOPK]), ALU.mult))
                link(dve.tensor_scalar(IDX[:, t, :], EX[:, 0, :], loff[:, 0:1], None, ALU.add), idx_done)
            return best_of_list, best_of_pairs, gates_in, experts_of

        with ExitStack() as load:
            def lb(name, shape, dt=F32):
                return load.enter_context(nc.sbuf_tensor(name, shape, dt))

            QP = lb("QP", [P, 2 * PH, S])
            SKT = lb("SKT", [P, 2 * PH, P])
            WQ = lb("WQ", [P, 2, KD, 512])
            SK = SC[:, T - 1, :, :]
            wq_in = [sem_of(f"wq_in{i}") for i in range(2)]
            sk_in, sk_tp, sk_ev, q_mm, s_mm = (sem_of(f"r_{s}") for s in ("sk_in", "sk_tp", "sk_ev", "q_mm", "s_mm"))
            q_ev, s_ev = sem_of("r_q_ev"), sem_of("r_s_ev")
            passes = [(0, P), (P, S)]
            with nc.Block() as block:
                @block.sync
                def _(sp):
                    keys = a["peer_subkeys"][layer].rearrange("h j k d -> k (h j) d")
                    for i in range(2 * PH):
                        sp.dma_start(SK[:, i, :], keys[:, i, :]).then_inc(sk_in, 16)
                    for n in range(8):
                        if n >= 2:
                            sp.wait_ge(q_mm, 4 * (n - 1))
                        lo = n % 4 * 512
                        sp.dma_start(WQ[:, n % 2, :, :], a["peer_wq"][layer, :, lo:lo + 512]
                                     .rearrange("(k p) n -> p k n", p=P)).then_inc(wq_in[n % 2], 16)

                @block.tensor
                def _(pe):
                    pe.wait_ge(sk_in, 16 * 2 * PH)
                    for g in range(4):
                        for i in range(4):
                            last = pe.transpose(PS[:, 4 + g, i * P:(i + 1) * P], SK[:, 4 * g + i, :], eye[:, :])
                        last.then_inc(sk_tp, 1)
                    for i in range(32):
                        j = i % 16
                        lo, hi = passes[i // 16]
                        pe.wait_ge(wq_in[i // 4 % 2], 16 * (i // 8 + 1))
                        if i >= 4:
                            pe.wait_ge(q_ev, i - 3)
                        for k in range(KD):
                            last = pe.matmul(PS[:, j % 4, 0:hi - lo], WQ[:, j // 4 % 2, k, (j % 4) * P:(j % 4 + 1) * P],
                                             HT[:, k, lo:hi], start=(k == 0), stop=(k == KD - 1))
                        last.then_inc(q_mm, 1)
                        if j < 15:
                            continue
                        pe.wait_ge(sk_ev, 4)
                        pe.wait_ge(q_ev, i + 1)
                        for t in range(lo // P, hi // P):
                            bank = 4 * ((t + 1) % 2)
                            if t >= 2:
                                pe.wait_ge(s_ev, t - 1)
                            for j in range(16):
                                last = pe.matmul(PS[:, bank + j // 4, (j % 4) * P:(j % 4 + 1) * P],
                                                 QP[:, j, t * P:(t + 1) * P], SKT[:, j, :], start=True, stop=True)
                            last.then_inc(s_mm, 1)

                @block.scalar
                def _(act):
                    for g in range(4):
                        act.wait_ge(sk_tp, g + 1)
                        act.activation(SKT[:, 4 * g:4 * g + 4, :].rearrange("p a b -> p (a b)"), PS[:, 4 + g, :],
                                       ACT.Copy).then_inc(sk_ev, 1)
                    for i in range(32):
                        j = i % 16
                        lo, hi = passes[i // 16]
                        act.wait_ge(q_mm, i + 1)
                        act.activation(QP[:, j, lo:hi], PS[:, j % 4, 0:hi - lo], ACT.Copy).then_inc(q_ev, 1)
                        if j < 15:
                            continue
                        for t in range(lo // P, hi // P):
                            if t == 2:
                                act.wait_ge(g_in, 1)
                                act.activation(GATE[:, 0, :], GATE[:, 0, :], ACT.Exp).then_inc(g_exp, 1)
                                act.wait_ge(idx_done, 1)
                            act.wait_ge(s_mm, t + 1)
                            bank = 4 * ((t + 1) % 2)
                            act.activation(SC[:, t, :, :].rearrange("p (b j) k -> p b (j k)", b=4),
                                           PS[:, bank:bank + 4, :], ACT.Copy).then_inc(s_ev, 1)

                @block.vector
                def _(dve):
                    link.eng = dve
                    (best_of_list, best_of_pairs, gates_in, experts_of) = router(dve, first)
                    dve.wait_ge(sk_ev, 4)
                    dve.wait_ge(s_ev, 1)
                    with dve.Fori(0, PH) as h:
                        for j in range(2):
                            best_of_list(0, h * 2 + j)
                    with dve.Fori(0, PH) as h:
                        best_of_pairs(h)
                    gates_in(0)
                    experts_of(0)

        rows = sb("rows_ring", [P, RING, D])
        nxt = sb("idx_next", [P, 2, RING], U32)
        W = sb("W", [P, 2, SLOTS])
        ACC = sb("ACC", [P, D])
        DG = sb("DIAG", [P, RING // 2, P])
        ZERO = sb("ZERO", [P, P])
        tabs = [a["peer_u"].rearrange("l e d -> (l e) d"), a["peer_v"].rearrange("l e d -> (l e) d")]
        GROUPS_ = SLOTS // RING
        tile_groups = 2 * GROUPS_

        def group_of(t, side, g):
            return (layer * T + t) * tile_groups + side * GROUPS_ + g

        with nc.Block() as block:
            @block.scalar
            def _(act):
                def stage(t, side, g, half):
                    act.activation(nxt[:, half, :], IDX[:, t, bass.ds(g * RING, RING)], ACT.Copy).then_inc(staged, 1)

                def group_used(n):
                    act.wait_ge(ring_free[RING - 2], n + 2)
                    act.wait_ge(ring_free[RING - 1], n + 2)

                def gates(t):
                    act.wait_ge(g_in, t + 1)
                    act.activation(GATE[:, t, :], GATE[:, t, :], ACT.Exp).then_inc(g_exp, 1)

                def diags(t, g):
                    for b in range(1, RING, 2):
                        act.activation(DG[:, b // 2, :], eye[:, :], ACT.Copy,
                                       scale=W[:, 0, bass.ds(g * RING + b, 1)]).then_inc(diag_ready, 1)

                stage(0, 0, 0, 0)
                stage(0, 0, 1, 1)
                for t in range(T):
                    with act.Fori(0, GROUPS_ // 2 - 1) as g2:
                        for half in range(2):
                            group_used(group_of(t, 0, g2 * 2 + half))
                            stage(t, 0, g2 * 2 + half + 2, half)
                    for half in range(2):
                        group_used(group_of(t, 0, GROUPS_ - 2 + half))
                        stage(t, 1, half, half)
                    act.wait_ge(act_ready, layer * T + t + 1)
                    act.activation(W[:, 1, :], W[:, 1, :], ACT.Exp).then_inc(peer_exp, 1)
                    act.wait_ge(gated, layer * T + t + 1)
                    half_way = GROUPS_ // 4
                    for lo, hi in ((0, half_way), (half_way, GROUPS_ // 2 - 1)):
                        with act.Fori(lo, hi) as g2:
                            for half in range(2):
                                diags(t, g2 * 2 + half)
                                group_used(group_of(t, 1, g2 * 2 + half))
                                stage(t, 1, g2 * 2 + half + 2, half)
                        if lo == 0 and t + 1 < T:
                            gates(t + 1)
                    for half in range(2):
                        diags(t, GROUPS_ - 2 + half)
                        if t + 1 < T or half == 0:
                            group_used(group_of(t, 1, GROUPS_ - 2 + half))
                        if t + 1 < T:
                            if half == 0:
                                act.wait_ge(idx_done, t + 2)
                            stage(t + 1, 0, half, half)

            @block.gpsimd
            def _(pool):
                with pool.Fori(0, T) as t:
                    for side in range(2):
                        with pool.Fori(0, GROUPS_ // 2) as g2:
                            for half in range(2):
                                n = group_of(t, side, g2 * 2 + half)
                                pool.wait_ge(staged, n + 1)
                                for b in range(RING):
                                    pool.wait_ge(ring_free[b], n + 1)
                                    pool.sem_inc(ring_taken, 1)
                                    pool.indirect_dma_start(
                                        out=rows[:, b, :], out_offset=None, in_=tabs[side],
                                        in_offset=bass.IndirectOffsetOnAxis(ap=nxt[:, half, b:b + 1], axis=0))\
                                        .then_inc(ring_in[b], 16)

            @block.tensor
            def _(pe):
                pe.wait_ge(zeroed, layer + 1)
                for t in range(T):
                    bank = 2 * (t % 2)
                    if t >= 2:
                        pe.wait_ge(out_step, layer * T + t - 1)
                    for c in range(2):
                        pe.matmul(PS[:, bank + c, :], ZERO[:, :], X[:, t, c * 512:(c + 1) * 512], start=True,
                                  stop=False, skip_group_check=True)
                    with pe.Fori(0, GROUPS_) as g:
                        for b in range(1, RING, 2):
                            n = group_of(t, 1, g)
                            pe.wait_ge(ring_in[b], 16 * (n + 1))
                            pe.wait_ge(diag_ready, ((layer * T + t) * GROUPS_ + g) * (RING // 2) + b // 2 + 1)
                            for c in range(2):
                                last = pe.matmul(PS[:, bank + c, :], DG[:, b // 2, :],
                                                 rows[:, b, c * 512:(c + 1) * 512], start=False, stop=False,
                                                 skip_group_check=True)
                            last.then_inc(ring_free[b], 1)
                    for c in range(2):
                        last = pe.matmul(PS[:, bank + c, :], ZERO[:, :], X[:, t, c * 512:(c + 1) * 512], start=False,
                                         stop=True, skip_group_check=True)
                    last.then_inc(pe_sum, 1)

            @block.vector
            def _(dve):
                link.eng = dve
                dve.memset(ZERO[:, :], 0.0).then_inc(zeroed, 1)

                (best_of_list, best_of_pairs, gates_in, experts_of) = router(dve, later)

                for t in range(T):
                    with dve.Fori(0, GROUPS_) as g:
                        n = group_of(t, 0, g)
                        for b in range(RING):
                            dve.wait_ge(ring_in[b], 16 * (n + 1))
                            dve.scalar_tensor_tensor(rows[:, b, :], rows[:, b, :], 1.0, H[:, t, :], ALU.mult, ALU.mult,
                                                     accum_out=W[:, 0, bass.ds(g * RING + b, 1)])\
                                .then_inc(ring_free[b], 1)
                            if t + 1 < T and b % 8 == 7:
                                j = g * 2 + b // 8
                                best_of_list(t + 1, j)
                    dve.wait_ge(ring_free[RING - 1], group_of(t, 1, 0) + 1)
                    plink = Turn(dve, peer_step)
                    y, g_ = W[:, 0, :], W[:, 1, :]
                    gelu_terms(plink, dve, y, g_)
                    dve.sem_inc(act_ready, 1)
                    plink(dve.memset(ACC[:, :], 0.0))
                    plink(dve.tensor_tensor(y, y, GATE[:, t, :], ALU.mult))
                    dve.wait_ge(peer_exp, layer * T + t + 1)
                    plink(dve.tensor_scalar(g_, g_, 1.0, None, ALU.add))
                    plink(dve.reciprocal(g_, g_))
                    dve.tensor_tensor(y, y, g_, ALU.mult).then_inc(gated, 1)

                    half_way = GROUPS_ // 2
                    for part in range(2):
                        with dve.Fori(part * half_way, (part + 1) * half_way) as g:
                            n = group_of(t, 1, g)
                            dve.wait_ge(gated, layer * T + t + 1)
                            for b in range(0, RING, 2):
                                dve.wait_ge(ring_in[b], 16 * (n + 1))
                                dve.wait_ge(ring_free[b - 2 if b else RING - 2], n + (2 if b else 1))
                                dve.scalar_tensor_tensor(ACC[:, :], rows[:, b, :], W[:, 0, bass.ds(g * RING + b, 1)],
                                                         ACC[:, :], ALU.mult, ALU.add).then_inc(ring_free[b], 1)
                                if t + 1 < T and part == 0 and b % 8 == 6:
                                    h = g * 2 + b // 8
                                    best_of_pairs(h)
                        if t + 1 < T and part == 0:
                            gates_in(t + 1)
                            experts_of(t + 1)
                    dve.wait_ge(ring_free[RING - 2], group_of(t + 1, 0, 0) + 1)
                    dve.wait_ge(pe_sum, layer * T + t + 1)
                    bank = 2 * (t % 2)
                    dve.tensor_tensor(ACC[:, :], ACC[:, :], PS[:, bank:bank + 2, :].rearrange("p b c -> p (b c)"),
                                      ALU.add).then_inc(out_step, 1)
                    dve.wait_ge(out_step, layer * T + t + 1)
                    plink(dve.tensor_tensor(ACC[:, :], ACC[:, :], MOD[:, 5, :], ALU.mult))
                    plink(dve.tensor_tensor(X[:, t, :], X[:, t, :], ACC[:, :], ALU.add))
                    plink.done()
                link(dve.tensor_scalar(loff[:, :], loff[:, :], float(EXPERTS), None, ALU.add))


def build(nc, a, out):
    outer = ExitStack()
    with outer:
        def tensors(stack):
            def sb(name, shape, dt=F32):
                return stack.enter_context(nc.sbuf_tensor(name, shape, dt))
            return sb

        sems = []

        def sem(name, keep=False):
            s = outer.enter_context(nc.semaphore(name))
            if not keep:
                sems.append(s)
            return s

        sb = tensors(outer)
        X = sb("X", [P, T, D])
        MOD = sb("MOD", [P, 6, D])
        H = sb("H", [P, T, D])
        HT = sb("HT", [P, KD, S])
        BM = sb("BM", [P, HEADS + 1, S])
        eye = sb("eye", [P, P])
        cosT = sb("cosT", [P, T, 16])
        sinT = sb("sinT", [P, T, 16])
        blk = sb("blk", [P, SJ, 8])
        rowpar = sb("rowpar", [P, P])
        means = sb("means", [P, 16])
        lst = sb("lst", [P, TOPK])
        CB = sb("CB", [P, KD, P])
        loff = sb("loff", [P, 1])
        RS = sb("RS", [P, 96])
        V0 = sb("V0", [P, 96])
        NT = sb("NT", [P, 2, 96])
        PS = outer.enter_context(nc.psum_tensor("PS", [P, 8, 512], F32))
        toep = nc.dram_tensor("toep", (HEADS + 1, TOEP), F32, kind="Internal").ap()

        dve_step = sem("dve_step")
        act_step = sem("act_step")
        pool_step = sem("pool_step")
        dve_layer = sem("dve_layer", keep=True)
        act_layer = sem("act_layer", keep=True)

        def rsqrt(link, n, terms=3):
            v, y, t = V0[:, 0:n], RS[:, 0:n], NT[:, 0, 0:n]
            dve = nc.vector
            link(dve.tensor_scalar(t.bitcast(I32), v.bitcast(I32), 1, None, ALU.logical_shift_right))
            link(dve.tensor_scalar(y.bitcast(I32), t.bitcast(I32), -1.0, float(0x5F3759DF), ALU.mult, ALU.add))
            for _ in range(terms):
                link(dve.tensor_tensor(t, y, y, ALU.mult))
                link(dve.tensor_tensor(t, t, v, ALU.mult))
                link(dve.tensor_scalar(t, t, -0.5, 1.5, ALU.mult, ALU.add))
                link(dve.tensor_tensor(y, y, t, ALU.mult))

        with ExitStack() as st:
            sb = tensors(st)
            rows = sb("rows", [BUCKETS + 2, TOEP])
            sel = sb("sel", [BUCKETS + 2, HEADS + 1])
            flip = sb("flip", [P, P])
            ccol = sb("ccol", [P, 3, KD])
            wr = sb("wr", [HEADS + 1, TOEP])
            BMr = sb("BMr", [P, HEADS + 1, S])
            loads = sem("once_loads")
            sel_in = sem("sel_in")
            rel_in = sem("rel_in")
            bias_rows = sem("bias_rows")
            bias_copied = sem("bias_copied")
            bias_stored = sem("bias_stored")
            bias_back = sem("bias_back")
            bias_flipped = sem("bias_flipped")
            exp_c = sem("exp_c")
            n_loads = 11
            with nc.Block() as block:
                @block.sync
                def _(sp):
                    sp.dma_start(sel[:, :], a["c_sel"]).then_inc(sel_in, 16)
                    sp.dma_start(ccol[:, 0, :], a["c"].rearrange("a (k p) -> p (a k)", p=P),
                                 allow_slow_non_contiguous=True).then_inc(loads, 16)
                    sp.dma_start(rows[:, :], a["c_rows"]).then_inc(loads, 16)
                    sp.dma_start(flip[:, :], a["c_flip"]).then_inc(loads, 16)
                    sp.dma_start(eye[:, :], a["c_eye"]).then_inc(loads, 16)
                    sp.dma_start(cosT[:, :, :], a["c_cos"].rearrange("(t p) f -> p t f", p=P)).then_inc(loads, 16)
                    sp.dma_start(sinT[:, :, :], a["c_sin"].rearrange("(t p) f -> p t f", p=P)).then_inc(loads, 16)
                    sp.dma_start(blk[:, :, :], a["c_blk"].rearrange("p (j b) -> p j b", b=8)).then_inc(loads, 16)
                    sp.dma_start(rowpar[:, :], a["c_rowpar"]).then_inc(loads, 16)
                    sp.dma_start(means[:, :], a["c_means"]).then_inc(loads, 16)
                    sp.dma_start(lst[:, :], a["c_list"]).then_inc(loads, 16)
                    sp.dma_start(X[:, :, :], a["x"].rearrange("a (t p) d -> p (a t) d", p=P)).then_inc(loads, 16)
                    sp.wait_ge(sel_in, 16)
                    sp.dma_start(sel[0:BUCKETS, 0:HEADS], a["rel_bias"].rearrange("h b -> b h"),
                                 allow_slow_non_contiguous=True).then_inc(rel_in, 16)
                    sp.wait_ge(bias_copied, 2)
                    sp.dma_start(toep, wr[:, :]).then_inc(bias_stored, 16)
                    sp.wait_ge(bias_stored, 16)
                    for h in range(HEADS + 1):
                        shifted = bass.AP(toep.tensor, h * TOEP, [[1, P], [1, S]])
                        sp.dma_start(BMr[:, h, :], shifted).then_inc(bias_back, 16)
                    sp.wait_ge(bias_back, 16 * (HEADS + 1))

                @block.tensor
                def _(pe):
                    pe.wait_ge(loads, 16 * n_loads)
                    pe.wait_ge(rel_in, 16)
                    for half in range(2):
                        pe.matmul(PS[0:HEADS + 1, half, 0:320], sel[:, :], rows[:, half * 320:half * 320 + 320],
                                  start=True, stop=True).then_inc(bias_rows, 1)
                    pe.wait_ge(bias_back, 16 * (HEADS + 1))
                    for h in range(HEADS + 1):
                        pe.matmul(PS[:, 1 + h, :], flip[:, :], BMr[:, h, :], start=True, stop=True)\
                            .then_inc(bias_flipped, 1)

                @block.scalar
                def _(act):
                    act.wait_ge(loads, 16 * n_loads)
                    act.activation(ccol[:, 1, :], ccol[:, 0, :], ACT.Exp, scale=-1.0).then_inc(exp_c, 1)

                @block.vector
                def _(dve):
                    link = Link(dve, dve_step)
                    for half in range(2):
                        dve.wait_ge(bias_rows, half + 1)
                        dve.tensor_copy(wr[:, half * 320:half * 320 + 320], PS[0:HEADS + 1, half, 0:320])\
                            .then_inc(bias_copied, 1)
                    dve.wait_ge(exp_c, 1)
                    link(dve.tensor_scalar(ccol[:, 1, :], ccol[:, 1, :], 1.0, None, ALU.add))
                    link(dve.reciprocal(ccol[:, 2, :], ccol[:, 1, :]))
                    link(dve.tensor_tensor(ccol[:, 0, :], ccol[:, 0, :], ccol[:, 2, :], ALU.mult))
                    link(dve.tensor_copy(CB[:, :, :], ccol[:, 0, :].unsqueeze(2).to_broadcast([P, KD, P])))
                    link(dve.memset(loff[:, :], 0.0))
                    for h in range(HEADS + 1):
                        dve.wait_ge(bias_flipped, h + 1)
                        link(dve.tensor_copy(BM[:, h, :], PS[:, 1 + h, :]))

        def clear_all():
            with nc.Block() as block:
                @block.vector
                def _(dve):
                    for s in sems:
                        dve.sem_clear(s)

        clear_all()

        peer_sems = ([sem(f"ring_in{b}", keep=True) for b in range(RING)],
                     [sem(f"ring_free{b}", keep=True) for b in range(RING)],
                     *(sem(name, keep=True) for name in (
                         "ring_taken", "idx_staged", "act_ready", "gated", "out_step", "peer_step", "peer_exp",
                         "top_step", "diag_ready", "pe_sum", "zeroed")))
        with nc.Block() as block:
            @block.vector
            def _(dve):
                for free in peer_sems[1]:
                    dve.sem_inc(free, 1)

        wbuf_in = [sem(f"wbuf_in{i}") for i in range(2)]
        mod_mm = sem("mod_mm")
        mod_ev = sem("mod_ev")
        mod_loads = sem("mod_loads")

        names = {}

        def named(name):
            if name not in names:
                names[name] = sem(name)
            return names[name]

        def norm_block(which, scale, shift):
            ss, hs, tp, ev = (named(f"n{which}_{s}") for s in ("sumsq", "h", "tp", "ev"))
            with nc.Block() as block:
                @block.scalar
                def _(act):
                    for t in range(T):
                        act.activation(H[:, t, :], X[:, t, :], ACT.Square, accum_out=V0[:, t:t + 1]).then_inc(ss, 1)
                    for t in range(T):
                        act.wait_ge(tp, t + 1)
                        b = 2 * (t % 2)
                        act.activation(HT[:, :, t * P:(t + 1) * P],
                                       PS[:, b:b + 2, :].rearrange("p b (k c) -> p (b k) c", c=P),
                                       ACT.Copy).then_inc(ev, 1)

                @block.vector
                def _(dve):
                    link.eng = dve
                    dve.wait_ge(ss, T)
                    link(dve.tensor_scalar(V0[:, 0:T], V0[:, 0:T], 1.0 / D, EPS, ALU.mult, ALU.add))
                    rsqrt(link, T)
                    for t in range(T):
                        link(dve.scalar_tensor_tensor(H[:, t, :], X[:, t, :], RS[:, t:t + 1], MOD[:, scale, :],
                                                      ALU.mult, ALU.mult))
                        link(dve.tensor_tensor(H[:, t, :], H[:, t, :], MOD[:, shift, :], ALU.add), hs)

                @block.tensor
                def _(pe):
                    for t in range(T):
                        pe.wait_ge(hs, t + 1)
                        if t >= 2:
                            pe.wait_ge(ev, t - 1)
                        for k in range(KD):
                            last = pe.transpose(PS[:, 2 * (t % 2) + k // 4, (k % 4) * P:(k % 4 + 1) * P],
                                                H[:, t, k * P:(k + 1) * P], eye[:, :])
                        last.then_inc(tp, 1)

        with nc.Fori(0, DEPTH) as layer:
            link = Link(nc.vector, dve_step)
            with ExitStack() as st:
                sb = tensors(st)
                WA = sb("WA", [P, 2, KD, 512])
                GB = sb("GB", [P, D])
                with nc.Block() as block:
                    @block.sync
                    def _(sp):
                        sp.dma_start(MOD[:, :, :].rearrange("p s d -> p (s d)"),
                                     a["b_ada"][layer, :].partition_broadcast(P)).then_inc(mod_loads, 16)
                        sp.dma_start(GB[:, :], a["norm1_gain"][layer, :].partition_broadcast(P)).then_inc(mod_loads, 16)
                        for n in range(4):
                            if n >= 2:
                                sp.wait_ge(mod_mm, n - 1)
                            sp.dma_start(WA[:, n % 2, :, :],
                                         a["w_ada"][layer, :, n * 512:(n + 1) * 512].rearrange("(k p) n -> p k n", p=P))\
                                .then_inc(wbuf_in[n % 2], 16)

                    @block.tensor
                    def _(pe):
                        for n in range(4):
                            pe.wait_ge(wbuf_in[n % 2], 16 * (n // 2 + 1))
                            if n >= 2:
                                pe.wait_ge(mod_ev, n - 1)
                            for k in range(KD):
                                last = pe.matmul(PS[:, n % 2, :], CB[:, k, :], WA[:, n % 2, k, :],
                                                 start=(k == 0), stop=(k == KD - 1))
                            last.then_inc(mod_mm, 1)

                    @block.vector
                    def _(dve):
                        link.eng = dve
                        dve.wait_ge(mod_loads, 32)
                        for n in range(4):
                            dve.wait_ge(mod_mm, n + 1)
                            m = MOD[:, n // 2, (n % 2) * 512:(n % 2 + 1) * 512]
                            link(dve.tensor_tensor(m, PS[:, n % 2, :], m, ALU.add), mod_ev)
                        link(dve.scalar_tensor_tensor(MOD[:, 1, :], MOD[:, 1, :], 1.0, GB[:, :], ALU.add, ALU.mult))

            norm_block(1, 1, 0)

            with ExitStack() as mix:
                sb = tensors(mix)
                PRJ = sb("PRJ", [P, T, COLS])
                wi_in = [named(f"wi_in{i}") for i in range(2)]
                pj_mm, pj_ev = named("pj_mm"), [named("pj_ev_act"), named("pj_ev_dve")]
                NCH = COLS // 4
                with ExitStack() as st:
                    WI = tensors(st)("WI", [P, 2, KD, NCH])
                    with nc.Block() as block:
                        @block.sync
                        def _(sp):
                            for n in range(4):
                                if n >= 2:
                                    sp.wait_ge(pj_mm, 4 * (n - 1))
                                sp.dma_start(WI[:, n % 2, :, :],
                                             a["w_in"][layer, :, n * NCH:(n + 1) * NCH]
                                             .rearrange("(k p) n -> p k n", p=P)).then_inc(wi_in[n % 2], 16)

                        @block.tensor
                        def _(pe):
                            for i in range(16):
                                n, t = i // 4, i % 4
                                pe.wait_ge(wi_in[n % 2], 16 * (n // 2 + 1))
                                if i >= 4:
                                    pe.wait_ge(pj_ev[i % 2], (i - 4) // 2 + 1)
                                for k in range(KD):
                                    last = pe.matmul(PS[:, i % 4, 0:NCH], HT[:, k, t * P:(t + 1) * P],
                                                     WI[:, n % 2, k, :], start=(k == 0), stop=(k == KD - 1))
                                last.then_inc(pj_mm, 1)

                        @block.scalar
                        def _(act):
                            for i in range(0, 16, 2):
                                n, t = i // 4, i % 4
                                act.wait_ge(pj_mm, i + 1)
                                act.activation(PRJ[:, t, n * NCH:(n + 1) * NCH], PS[:, i % 4, 0:NCH], ACT.Copy)\
                                    .then_inc(pj_ev[0], 1)

                        @block.vector
                        def _(dve):
                            for i in range(1, 16, 2):
                                n, t = i // 4, i % 4
                                dve.wait_ge(pj_mm, i + 1)
                                dve.tensor_copy(PRJ[:, t, n * NCH:(n + 1) * NCH], PS[:, i % 4, 0:NCH])\
                                    .then_inc(pj_ev[1], 1)

                s5_block(nc, a, layer, link, named, PS, PRJ, MOD, CB, H, HT, eye, blk, rowpar)
                attention(nc, a, layer, link, named, PS, PRJ, H, HT, eye, means, BM, cosT, sinT, RS, V0, rsqrt)

            with ExitStack() as st:
                sb = tensors(st)
                WO = sb("WO", [P, KD, D])
                MG = sb("MG", [P, D])
                TMP = sb("TMP", [P, 2, 512])
                GB2 = sb("GB2", [P, D])
                wo_in, ss, yn, tp, ev, mm, res = (named(f"out_{s}") for s in
                                                  ("w", "sumsq", "y", "tp", "ev", "mm", "res"))
                parts = [(0, SWA), (SWA, SWA + S5C), (SWA + S5C, D)]
                with nc.Block() as block:
                    @block.sync
                    def _(sp):
                        sp.dma_start(MG[:, :], a["mix_gain"][layer, :].partition_broadcast(P)).then_inc(wo_in, 16)
                        sp.dma_start(GB2[:, :], a["norm2_gain"][layer, :].partition_broadcast(P)).then_inc(wo_in, 16)
                        sp.dma_start(WO[:, :, :], a["w_out"][layer].rearrange("(k p) n -> p k n", p=P))\
                            .then_inc(wo_in, 16)

                    @block.scalar
                    def _(act):
                        for t in range(T):
                            for i, (lo, hi) in enumerate(parts):
                                act.activation(HT[:, 2 * t:2 * t + 2, :].rearrange("p a b -> p (a b)")[:, lo:hi],
                                               H[:, t, lo:hi], ACT.Square,
                                               accum_out=V0[:, 4 * i + t:4 * i + t + 1]).then_inc(ss, 1)
                        for t in range(T):
                            act.wait_ge(tp, t + 1)
                            b = 2 * (t % 2)
                            act.activation(HT[:, :, t * P:(t + 1) * P],
                                           PS[:, b:b + 2, :].rearrange("p b (k c) -> p (b k) c", c=P),
                                           ACT.Copy).then_inc(ev, 1)

                    @block.vector
                    def _(dve):
                        link.eng = dve
                        dve.wait_ge(ss, 3 * T)
                        for i, (lo, hi) in enumerate(parts):
                            link(dve.tensor_scalar(V0[:, 4 * i:4 * i + 4], V0[:, 4 * i:4 * i + 4],
                                                   1.0 / (hi - lo), EPS, ALU.mult, ALU.add))
                        rsqrt(link, 12)
                        dve.wait_ge(wo_in, 48)
                        for t in range(T):
                            for i, (lo, hi) in enumerate(parts):
                                link(dve.scalar_tensor_tensor(H[:, t, lo:hi], H[:, t, lo:hi],
                                                              RS[:, 4 * i + t:4 * i + t + 1], MG[:, lo:hi],
                                                              ALU.mult, ALU.mult), yn)
                        link(dve.scalar_tensor_tensor(MOD[:, 4, :], MOD[:, 4, :], 1.0, GB2[:, :], ALU.add, ALU.mult))
                        for i in range(8):
                            n, t = i // 4, i % 4
                            cols = slice(n * 512, (n + 1) * 512)
                            dve.wait_ge(mm, i + 1)
                            link(dve.tensor_tensor(TMP[:, i % 2, :], PS[:, 4 + i % 4, :], MOD[:, 2, cols],
                                                   ALU.mult), res)
                            link(dve.tensor_tensor(X[:, t, cols], X[:, t, cols], TMP[:, i % 2, :], ALU.add))

                    @block.tensor
                    def _(pe):
                        for t in range(T):
                            pe.wait_ge(yn, 3 * (t + 1))
                            if t >= 2:
                                pe.wait_ge(ev, t - 1)
                            for k in range(KD):
                                last = pe.transpose(PS[:, 2 * (t % 2) + k // 4, (k % 4) * P:(k % 4 + 1) * P],
                                                    H[:, t, k * P:(k + 1) * P], eye[:, :])
                            last.then_inc(tp, 1)
                        pe.wait_ge(wo_in, 48)
                        pe.wait_ge(ev, T)
                        for i in range(8):
                            n, t = i // 4, i % 4
                            if i >= 4:
                                pe.wait_ge(res, i - 3)
                            for k in range(KD):
                                last = pe.matmul(PS[:, 4 + i % 4, :], HT[:, k, t * P:(t + 1) * P],
                                                 WO[:, k, n * 512:(n + 1) * 512], start=(k == 0), stop=(k == KD - 1))
                            last.then_inc(mm, 1)

            norm_block(2, 4, 3)
            peer(nc, a, layer, link, named, PS, X, MOD, H, HT, eye, lst, loff, peer_sems)
            clear_all()

        stored = sem("stored")
        with nc.Block() as block:
            @block.sync
            def _(sp):
                sp.dma_start(out.rearrange("a (t p) d -> p (a t) d", p=P), X[:, :, :]).then_inc(stored, 16)
                sp.wait_ge(stored, 16)


INPUTS = ["x", "c", "w_in", "w_out", "mix_gain", "norm1_gain", "norm2_gain", "w_ada", "b_ada", "rel_bias",
          "swa_q_gain", "swa_k_gain", "mla_q_lora_gain", "mla_kv_lora_gain", "w_uq", "w_ukv", "mla_q_gain",
          "mla_k_gain", "s5_a_re", "s5_a_im", "s5_b_re", "s5_b_im", "s5_c_re", "s5_c_im", "s5_d", "s5_log_dt",
          "w_glu", "b_glu", "peer_wq", "peer_subkeys", "peer_u", "peer_v"]


def kernel(**inputs):
    import numpy as _np
    import concourse.bacc as _bacc
    from concourse import mybir as _mybir
    from concourse.bass_utils import run_bass_kernel_spmd as _run

    nc = _bacc.Bacc("TRN2", target_bir_lowering=False, num_devices=1)
    arrays, args = {}, {}
    for name, value in [(n, inputs[n]) for n in INPUTS] + list(constants().items()):
        v = _np.ascontiguousarray(value)
        arrays[f"in_{name}"] = v
        args[name] = nc.dram_tensor(f"in_{name}", v.shape, _mybir.dt.from_np(v.dtype), kind="ExternalInput").ap()
    out = nc.dram_tensor("out_0", (1, S, D), _mybir.dt.float32, kind="ExternalOutput").ap()
    build(nc, args, out)
    r = _run(nc, [arrays], core_ids=[0])
    return r.results[0]["out_0"]
```
